# Optimizing a Trainium2 kernel written in Bass

```python
import jax, jax.numpy as jnp
from jax import lax
import numpy as np

D_MODEL = 2048
BATCH = 1
SEQ = 256
DEPTH = 1

HEAD_DIM = 128
MOBA_HEADS = 8
MOBA_WIDTH = MOBA_HEADS * HEAD_DIM
MOBA_BLOCK = 256
MOBA_TOPK = 3
MOBA_QCHUNK = 32
DN_HEADS = 8
DN_WIDTH = DN_HEADS * HEAD_DIM
DN_CONV = 4
DN_CHUNK = 64
D_FF = 5632
FFN_CONV = 3
NORM_EPS = 1e-6
IN_SIZES = (MOBA_WIDTH, MOBA_WIDTH, MOBA_WIDTH, 3 * DN_WIDTH, DN_WIDTH, DN_HEADS, DN_HEADS, D_MODEL, D_MODEL)
IN_COLS = sum(IN_SIZES)

kernel_name = "hybrid_moba_gdn_convglu"

def rms_norm(x, gain):
    xf = x.astype(jnp.float32)
    y = xf * lax.rsqrt(jnp.mean(xf * xf, axis=-1, keepdims=True) + NORM_EPS)
    return (y * gain.astype(jnp.float32)).astype(x.dtype)

def l2_norm(x):
    xf = x.astype(jnp.float32)
    return xf * lax.rsqrt(jnp.sum(xf * xf, axis=-1, keepdims=True) + NORM_EPS)

def causal_dwconv(x, w):
    k_width = w.shape[0]
    s = x.shape[1]
    xp = jnp.pad(x, ((0, 0), (k_width - 1, 0), (0, 0)))
    y = xp[:, 0:s] * w[0]
    for i in range(1, k_width):
        y = y + xp[:, i:i + s] * w[i]
    return y

def moba_branch(q, k, v, q_gain, k_gain):
    b, s, _ = q.shape
    shp = (b, s, MOBA_HEADS, HEAD_DIM)
    q = rms_norm(q.reshape(shp), q_gain)
    k = rms_norm(k.reshape(shp), k_gain)
    v = v.reshape(shp)
    sp = -(-s // MOBA_BLOCK) * MOBA_BLOCK
    pad = ((0, 0), (0, sp - s), (0, 0), (0, 0))
    q, k, v = [jnp.pad(t, pad).transpose(0, 2, 1, 3) for t in (q, k, v)]
    nb = sp // MOBA_BLOCK
    topk = min(MOBA_TOPK, nb)
    k_blocks = k.reshape(b, MOBA_HEADS, nb, MOBA_BLOCK, HEAD_DIM)
    v_blocks = v.reshape(b, MOBA_HEADS, nb, MOBA_BLOCK, HEAD_DIM)
    k_mean = jnp.mean(k_blocks.astype(jnp.float32), axis=3)
    scale = HEAD_DIM ** -0.5
    gather = jax.vmap(jax.vmap(lambda blocks, idx: blocks[idx]))
    block_ids = jnp.arange(nb)
    q_offs = jnp.arange(MOBA_QCHUNK)
    k_offs = jnp.arange(MOBA_BLOCK)

    def chunk(c):
        start = c * MOBA_QCHUNK
        qc = lax.dynamic_slice_in_dim(q, start, MOBA_QCHUNK, axis=2)
        qblk = start // MOBA_BLOCK
        gate = jnp.einsum('bhqd,bhnd->bhqn', qc.astype(jnp.float32), k_mean)
        gate = jnp.where(block_ids < qblk, gate, -jnp.inf)
        _, idx = lax.top_k(gate, topk)
        valid = idx < qblk
        k_sel = gather(k_blocks, idx)
        v_sel = gather(v_blocks, idx)
        s_sel = jnp.einsum('bhqd,bhqnkd->bhqnk', qc, k_sel).astype(jnp.float32) * scale
        s_sel = jnp.where(valid[..., None], s_sel, -jnp.inf).reshape(b, MOBA_HEADS, MOBA_QCHUNK, topk * MOBA_BLOCK)
        k_own = lax.dynamic_slice_in_dim(k, qblk * MOBA_BLOCK, MOBA_BLOCK, axis=2)
        v_own = lax.dynamic_slice_in_dim(v, qblk * MOBA_BLOCK, MOBA_BLOCK, axis=2)
        s_own = jnp.einsum('bhqd,bhkd->bhqk', qc, k_own).astype(jnp.float32) * scale
        causal = (qblk * MOBA_BLOCK + k_offs)[None, :] <= (start + q_offs)[:, None]
        s_own = jnp.where(causal, s_own, -jnp.inf)
        p = jax.nn.softmax(jnp.concatenate([s_sel, s_own], axis=-1), axis=-1)
        p_sel = p[..., :topk * MOBA_BLOCK].reshape(b, MOBA_HEADS, MOBA_QCHUNK, topk, MOBA_BLOCK).astype(v.dtype)
        p_own = p[..., topk * MOBA_BLOCK:].astype(v.dtype)
        return (jnp.einsum('bhqnk,bhqnkd->bhqd', p_sel, v_sel)
                + jnp.einsum('bhqk,bhkd->bhqd', p_own, v_own))

    out = lax.map(chunk, jnp.arange(sp // MOBA_QCHUNK))
    out = out.transpose(1, 0, 3, 2, 4).reshape(b, sp, MOBA_WIDTH)
    return out[:, :s]

def chunk_gated_delta_rule(q, k, v, g, beta):
    b, s, h, dk = q.shape
    dv = v.shape[-1]
    c = DN_CHUNK
    nc = s // c
    q, k, v = [t.transpose(0, 2, 1, 3).reshape(b, h, nc, c, -1) for t in (q, k, v)]
    g, beta = [t.transpose(0, 2, 1).reshape(b, h, nc, c) for t in (g, beta)]
    G = jnp.cumsum(g, axis=-1)
    tril = jnp.tril(jnp.ones((c, c), bool))
    strict = jnp.tril(jnp.ones((c, c), bool), -1)
    decay = jnp.exp(jnp.where(tril, G[..., :, None] - G[..., None, :], -jnp.inf))
    kb = k * beta[..., None]
    m = jnp.einsum('bhnck,bhnsk->bhncs', kb, k) * decay
    lmat = jnp.where(strict, m, 0.0) + jnp.eye(c, dtype=m.dtype)
    u = lax.linalg.triangular_solve(lmat, v * beta[..., None], left_side=True, lower=True, unit_diagonal=True)
    w = lax.linalg.triangular_solve(lmat, kb * jnp.exp(G)[..., None], left_side=True, lower=True, unit_diagonal=True)
    attn = jnp.einsum('bhnck,bhnsk->bhncs', q, k) * decay
    qg = q * jnp.exp(G)[..., None]
    kd = k * jnp.exp(G[..., -1:] - G)[..., None]
    glast = jnp.exp(G[..., -1])
    xs = tuple(jnp.moveaxis(t, 2, 0) for t in (u, w, attn, qg, kd, glast))

    def step(state, inp):
        u_c, w_c, a_c, qg_c, kd_c, gl_c = inp
        v_new = u_c - jnp.einsum('bhck,bhkv->bhcv', w_c, state)
        o_c = jnp.einsum('bhck,bhkv->bhcv', qg_c, state) + jnp.einsum('bhcs,bhsv->bhcv', a_c, v_new)
        state = state * gl_c[..., None, None] + jnp.einsum('bhck,bhcv->bhkv', kd_c, v_new)
        return state, o_c

    state0 = jnp.zeros((b, h, dk, dv), jnp.float32)
    _, o = lax.scan(step, state0, xs)
    return o.transpose(1, 0, 3, 2, 4).reshape(b, s, h, dv)

def deltanet_branch(qkv, z, b_in, a_in, conv_w, a_log, dt_bias, out_gain):
    b, s, _ = qkv.shape
    qkv = jax.nn.silu(causal_dwconv(qkv, conv_w))
    q, k, v = jnp.split(qkv, 3, axis=-1)
    shp = (b, s, DN_HEADS, HEAD_DIM)
    q = l2_norm(q.reshape(shp)) * (HEAD_DIM ** -0.5)
    k = l2_norm(k.reshape(shp))
    v = v.reshape(shp).astype(jnp.float32)
    beta = jax.nn.sigmoid(b_in.astype(jnp.float32))
    g = -jnp.exp(a_log.astype(jnp.float32)) * jax.nn.softplus(a_in.astype(jnp.float32) + dt_bias.astype(jnp.float32))
    o = chunk_gated_delta_rule(q, k, v, g, beta)
    o = rms_norm(o, out_gain) * jax.nn.silu(z.reshape(shp).astype(jnp.float32))
    return o.reshape(b, s, DN_WIDTH).astype(qkv.dtype)

def conv_glu(h, w_in, conv_w, conv_b, w_down):
    gate, up = jnp.split(h @ w_in, 2, axis=-1)
    gate = causal_dwconv(gate, conv_w) + conv_b
    return (jax.nn.silu(gate) * up) @ w_down

def setup_inputs(seed: int = 0) -> dict:
    key = jax.random.key(seed)
    ks = jax.random.split(key, 20)

    def nrm(k, shape, scale):
        return jax.random.normal(k, shape, jnp.float32) * scale

    dt = jnp.exp(jax.random.uniform(ks[8], (DEPTH, DN_HEADS), jnp.float32, np.log(1e-3), np.log(1e-1)))
    return {
        "x": nrm(ks[0], (BATCH, SEQ, D_MODEL), 1.0),
        "attn_norm": 1.0 + nrm(ks[1], (DEPTH, D_MODEL), 0.02),
        "w_in": nrm(ks[2], (DEPTH, D_MODEL, IN_COLS), D_MODEL ** -0.5),
        "moba_q_norm": 1.0 + nrm(ks[3], (DEPTH, HEAD_DIM), 0.02),
        "moba_k_norm": 1.0 + nrm(ks[4], (DEPTH, HEAD_DIM), 0.02),
        "dn_conv": nrm(ks[5], (DEPTH, DN_CONV, 3 * DN_WIDTH), DN_CONV ** -0.5),
        "dn_a_log": jnp.log(jax.random.uniform(ks[6], (DEPTH, DN_HEADS), jnp.float32, 1.0, 16.0)),
        "dn_dt_bias": dt + jnp.log(-jnp.expm1(-dt)),
        "dn_out_norm": 1.0 + nrm(ks[7], (DEPTH, HEAD_DIM), 0.02),
        "w_branch_a": nrm(ks[9], (DEPTH, MOBA_WIDTH, D_MODEL), MOBA_WIDTH ** -0.5),
        "w_branch_b": nrm(ks[10], (DEPTH, DN_WIDTH, D_MODEL), DN_WIDTH ** -0.5),
        "w_out": nrm(ks[11], (DEPTH, D_MODEL, D_MODEL), D_MODEL ** -0.5),
        "ffn_norm": 1.0 + nrm(ks[12], (DEPTH, D_MODEL), 0.02),
        "w_ffn_in": nrm(ks[13], (DEPTH, D_MODEL, 2 * D_FF), D_MODEL ** -0.5),
        "ffn_conv": nrm(ks[14], (DEPTH, FFN_CONV, D_FF), FFN_CONV ** -0.5),
        "ffn_conv_bias": nrm(ks[15], (DEPTH, D_FF), 0.01),
        "w_ffn_down": nrm(ks[16], (DEPTH, D_FF, D_MODEL), D_FF ** -0.5),
    }

def reference(x, attn_norm, w_in, moba_q_norm, moba_k_norm, dn_conv, dn_a_log, dn_dt_bias, dn_out_norm,
              w_branch_a, w_branch_b, w_out, ffn_norm, w_ffn_in, ffn_conv, ffn_conv_bias, w_ffn_down):
    splits = [int(v) for v in np.cumsum(IN_SIZES)[:-1]]
    for l in range(DEPTH):
        h = rms_norm(x, attn_norm[l])
        proj = h @ w_in[l]
        mq, mk, mv, dqkv, dz, db, da, ga, gb = jnp.split(proj, splits, axis=-1)
        y_a = moba_branch(mq, mk, mv, moba_q_norm[l], moba_k_norm[l])
        y_b = deltanet_branch(dqkv, dz, db, da, dn_conv[l], dn_a_log[l], dn_dt_bias[l], dn_out_norm[l])
        merged = jax.nn.sigmoid(ga) * (y_a @ w_branch_a[l]) + jax.nn.sigmoid(gb) * (y_b @ w_branch_b[l])
        x = x + merged @ w_out[l]
        h = rms_norm(x, ffn_norm[l])
        x = x + conv_glu(h, w_ffn_in[l], ffn_conv[l], ffn_conv_bias[l], w_ffn_down[l])
    return x


_drawn_inputs = setup_inputs


def setup_inputs(seed=0):
    import zlib

    import numpy as np

    out = dict(_drawn_inputs(seed))
    spreads = {}
    factors = {'attn_norm': 4.456,
     'moba_q_norm': 8.0,
     'moba_k_norm': 8.0,
     'dn_out_norm': 7.611,
     'ffn_norm': 13.762,
     'ffn_conv_bias': 37.963}
    for name, (base, spread) in spreads.items():
        noise = np.random.default_rng([zlib.crc32(name.encode()), seed]).standard_normal(out[name].shape)
        drawn = base * np.exp(spread * noise) if base else spread * noise
        out[name] = __import__('jax').numpy.asarray(drawn.astype(out[name].dtype))
    for name, factor in factors.items():
        out[name] = (out[name] * factor).astype(out[name].dtype)
    return out
```

```python
from contextlib import ExitStack

import concourse.bass as bass
from concourse import mybir

P = 128
SEQ = 256
TOK = SEQ // P
D = 2048
KD = D // P
HEADS = 8
HD = 128
CHUNK = 64
NCH = SEQ // CHUNK
TAPS = 4
FF = 5632
KF = FF // P
FTAPS = 3
EPS = 1e-6
SCALE = HD ** -0.5

SLOTS = 4
SLAB = 1024
LEVELS = 6
AHEAD_HI, AHEAD_LO = 3, 2

T_IN1 = 0
T_IN2 = T_IN1 + 16
T_IN3 = T_IN2 + 12
T_MRG = T_IN3 + 16
T_OUT = T_MRG + 8
T_FFN = T_OUT + 8
T_DWN = T_FFN + 44
TURNS = T_DWN + 22
U_IN1, U_IN2, U_IN3, U_MRG, U_OUT, U_FFN, U_DWN = 0, 8, 12, 20, 28, 30, 52

C_ID, C_UP, C_SAME, C_HALF, C_LEVEL, C_CAUSAL = 0, 128, 256, 384, 640, 1408
C_ALL = 1792
S_ATTN = 0
S_FFN = S_ATTN + KD
S_QG = S_FFN + KD
S_KG = S_QG + 1
S_OG = S_KG + 1
S_ALOG = S_OG + 1
S_DT = S_ALOG + HEADS
S_CONV = S_DT + HEADS
S_FCONV = S_CONV + 3 * HEADS * TAPS
S_FBIAS = S_FCONV + KF * FTAPS
S_ALL = S_FBIAS + KF

F32 = mybir.dt.float32
F32R = mybir.dt.float32r
ACT = mybir.ActivationFunctionType
ALU = mybir.AluOpType
AX_X = mybir.AxisListType.X


def layer(nc, x, stream, w_ba, consts, small, out):
    with ExitStack() as ctx:
        def sb(name, shape, dt=F32):
            return ctx.enter_context(nc.sbuf_tensor(name, shape, dt))

        def sem(name):
            return ctx.enter_context(nc.semaphore(name))

        con = sb("constants", [P, C_ALL])
        par = sb("parameters", [P, S_ALL])
        raw = sb("w_raw", [P, SLOTS, SLAB])
        whi = sb("w_hi", [P, SLOTS, SLAB], F32R)
        wlo = sb("w_lo", [P, SLOTS, SLAB], F32R)
        hs = sb("act_split", [P, KD, 2, SEQ], F32R)
        half = sb("second_half", [P, 3, 2, SEQ])
        rstat = sb("row_stat", [P, 8, TOK])
        ident = con[:, C_ID:C_ID + P]

        def at_once(groups):
            made = []
            for group in groups:
                with ExitStack() as inner:
                    made.append([inner.enter_context(nc.sbuf_tensor(n, s, d)) for n, s, d in group])
            return made

        mixer = ExitStack()
        z = mixer.enter_context(nc.sbuf_tensor("z", [P, HEADS, SEQ], F32))
        ya = mixer.enter_context(nc.sbuf_tensor("y_moba", [P, HEADS, 2, SEQ], F32R))
        (dn,), (yb,) = at_once([[("dn_qkv", [P, HEADS, 3, SEQ], F32)], [("y_dn", [P, HEADS, 3, SEQ], F32R)]])
        mixer.enter_context(nc.sbuf_tensor("dn_place", [P, HEADS, 3, SEQ], F32))
        (xt,), (qkv,), (gates,) = at_once([[("x_tokens", [P, TOK, D], F32)],
                                           [("moba_qkv", [P, 3 * HEADS, SEQ], F32)],
                                           [("gates", [P, 2 * KD, SEQ], F32)]])
        mixer.enter_context(nc.sbuf_tensor("gates_place", [P, 2 * KD, SEQ], F32))
        gcol = mixer.enter_context(nc.sbuf_tensor("gate_columns", [P, TOK, 6, HEADS], F32))
        glast = mixer.enter_context(nc.sbuf_tensor("chunk_decay", [P, NCH, HEADS], F32))
        ones = mixer.enter_context(nc.sbuf_tensor("ones", [P, P], F32))
        moba_set = [("m_sq", [P, 2, SEQ], F32), ("m_rs", [P, 2, SEQ], F32), ("m_qn", [P, SEQ], F32),
                    ("m_kn", [P, SEQ], F32), ("m_v", [P, SEQ], F32), ("m_s", [P, 3 * P], F32),
                    ("m_mx", [P, 8], F32), ("m_pt", [P, 3 * P], F32), ("m_vt", [P, TOK, P], F32),
                    ("conv_in", [P, 2, TAPS - 1 + SEQ], F32), ("conv_acc", [P, 2, SEQ], F32)]
        dn_set = [("d_sq", [P, 2, SEQ], F32), ("d_qn", [P, SEQ], F32), ("d_kn", [P, SEQ], F32),
                  ("d_v", [P, SEQ], F32), ("d_cast", [P, 2, TOK, P], F32), ("d_kb", [P, SEQ], F32),
                  ("d_e", [P, TOK, P], F32), ("d_qg", [P, SEQ], F32), ("d_lv", [P, LEVELS, TOK, P], F32),
                  ("d_tu", [P, 2, TOK, P], F32), ("d_p", [P, TOK, P], F32), ("d_vb", [P, TOK, P], F32),
                  ("d_kbg", [P, TOK, P], F32), ("d_kd", [P, TOK, P], F32), ("d_uw", [P, 2, TOK, P], F32),
                  ("d_at", [P, TOK, P], F32), ("d_vn", [P, TOK, P], F32),
                  ("d_state", [P, P], F32)]
        start_set = [("wba", [P, KD, 2 * HEADS], F32), ("wba_hi", [P, KD, 2 * HEADS], F32R),
                     ("wba_lo", [P, KD, 2 * HEADS], F32R), ("gt", [P, 6, TOK, HEADS], F32)]
        m_all, d_all, s_all = at_once([moba_set, dn_set, start_set])
        m_sq, m_rs, m_qn, m_kn, m_v, m_s, m_mx, m_pt, m_vt, cin, cacc = m_all
        (d_sq, d_qn, d_kn, d_v, d_cast, d_kb, d_e, d_qg, d_lv, d_tu, d_p, d_vb, d_kbg, d_kd, d_uw, d_at, d_vn,
         d_state) = d_all
        wba, wbah, wbal, gt = s_all
        mixer.close()
        x1 = sb("residual", [P, TOK, D])
        (scaled,), (act_s,) = at_once([[("x1_scaled", [P, TOK, D], F32)], [("hidden_split", [P, KF, 2, SEQ], F32R)]])
        sb("hidden_place", [P, KF, 2, SEQ])
        fin = sb("ffn_conv_in", [P, 2, FTAPS - 1 + SEQ])
        facc = sb("ffn_acc", [P, 2, SEQ])
        mg = z[:, :, :].rearrange("p (a c) t -> p a (c t)", c=2)

        ps = ctx.enter_context(nc.psum_tensor("ps", [P, 8, 512], F32))

        def pair(p):
            return ps[:, 2 * p:2 * p + 2, :].rearrange("p c (h t) -> p c h t", h=2)

        raw_loaded = [sem(f"raw_loaded{s}") for s in range(SLOTS)]
        hi_ready, lo_ready = sem("hi_ready"), sem("lo_ready")
        slabs_used = sem("slabs_used")
        pair_free = [sem(f"pair_free{p}") for p in range(3)]
        half_copied = [sem(f"half_copied{p}") for p in range(3)]
        x_loaded, tables_loaded, x1_loaded = sem("x_loaded"), sem("tables_loaded"), sem("x1_loaded")
        ones_set = sem("ones_set")
        row_sq, row_log, row_rstd, row_scaled = sem("row_sq"), sem("row_log"), sem("row_rstd"), sem("row_scaled")
        turned, hi_made, lo_made = sem("turned"), sem("hi_made"), sem("lo_made")
        ba_hi, ba_lo, ba_done = sem("ba_hi"), sem("ba_lo"), sem("ba_done")
        gate_v, gate_a, gate_sums, gates_ready = sem("gate_v"), sem("gate_a"), sem("gate_sums"), sem("gates_ready")
        names = ("m_free m_squares m_ssq m_log m_rstd m_qn_ready m_v_ready m_scores m_vturned m_masked m_max m_bias "
                 "m_exp m_rinv m_prob m_pturned m_pt_ready m_vt_ready m_out m_hi m_head_done "
                 "c_zero c_tap c_acc c_sum silu_done "
                 "d_free d_squares d_ssq d_log d_rstd d_cast_ready d_v_ready d_norm d_rows d_tok d_kb_ready d_prod "
                 "d_arg d_exp d_egrow d_qg_ready d_incl d_amat d_attn d_levels d_vb_ready d_kbg_ready d_kd_ready "
                 "d_u1 d_l0 d_tu_ready d_p_done d_p_ready d_tu_done d_uw d_u_ready "
                 "d_ws d_vn_ready d_okv d_state_ready d_osq d_ossq d_olog d_orstd d_on d_y d_yhi d_head_done "
                 "g_sig g_mul g_merged g_hi merged "
                 "f_zero f_tap f_acc f_silu f_prod f_hi hidden_ready "
                 "x1_added x1_sq stat_sum y_added y_stored last_stored").split()
        sg = {n: sem(n) for n in names}

        block = ctx.enter_context(nc.Block())

        def ahead(turn, s, by):
            return turn + (s + by) // SLOTS, (s + by) % SLOTS

        def cast(act, turn, s):
            turn, s = ahead(turn, s, AHEAD_HI)
            act.wait_ge(raw_loaded[s], (turn + 1) * 16)
            act.wait_ge(slabs_used, turn * SLOTS + s + 1)
            act.activation(whi[:, s], raw[:, s], ACT.Copy).then_inc(hi_ready, 1)

        def split(dve, turn, s):
            turn, s = ahead(turn, s, AHEAD_LO)
            dve.wait_ge(hi_ready, turn * SLOTS + s + 1)
            dve.tensor_tensor(wlo[:, s], raw[:, s], whi[:, s].bitcast(F32), ALU.subtract).then_inc(lo_ready, 1)

        def channel_unit(pe, turn, s, k, p, use, xs, kx, first, last):
            if k == 0:
                pe.wait_ge(lo_ready, turn * SLOTS + s + 1)
            if first:
                pe.wait_ge(pair_free[p], use + 1)
            both = xs[:, kx, 0:2, :].rearrange("p a t -> p (a t)")
            for c in range(2):
                at = k * 256 + c * P
                bank = ps[:, 2 * p + c, :]

                def lo_product():
                    return pe.matmul(bank[:, 0:SEQ], wlo[:, s, at:at + P], xs[:, kx, 0, :], start=False, stop=False,
                                     skip_group_check=True)
                if first:
                    pe.matmul(bank, whi[:, s, at:at + P], both, start=True, stop=False)
                    mm = lo_product()
                else:
                    lo_product()
                    mm = pe.matmul(bank, whi[:, s, at:at + P], both, start=False, stop=last)
            if k == 3:
                mm.then_inc(slabs_used, 1)

        def channel_group(pe, turn, p, use, xs, slots=(0, 1, 2, 3)):
            n = 4 * len(slots)
            for j in range(n):
                channel_unit(pe, turn, slots[j // 4], j % 4, p, use, xs, j, j == 0, j == n - 1)

        def multiplied(eng, turn, s=SLOTS - 1):
            eng.wait_ge(slabs_used, SLOTS + turn * SLOTS + s + 1)

        def read_out(eng, p, use):
            eng.wait_ge(pair_free[p], use + 2)

        def copy_half(act, p, turn, s=SLOTS - 1):
            multiplied(act, turn, s)
            act.activation(half[:, p], pair(p)[:, :, 1, :], ACT.Copy).then_inc(half_copied[p], 1)

        def add_halves(dve, p, use, dest, without=0):
            dve.wait_ge(half_copied[p], use - without + 1)
            return dve.tensor_tensor(dest, pair(p)[:, :, 0, :], half[:, p], ALU.add).then_inc(pair_free[p], 1)

        def token_slab(pe, turn, s, p, use, xs, kx, first, last):
            pe.wait_ge(lo_ready, turn * SLOTS + s + 1)
            if first:
                pe.wait_ge(pair_free[p], use + 1)
            for k in range(2):
                w_h, w_l = whi[:, s, k * 512:(k + 1) * 512], wlo[:, s, k * 512:(k + 1) * 512]
                for t in range(TOK):
                    bank = ps[:, 2 * p + t, :]
                    x_h, x_l = xs[:, kx + k, 0, t * P:(t + 1) * P], xs[:, kx + k, 1, t * P:(t + 1) * P]
                    pe.matmul(bank, x_h, w_l, start=first and k == 0, stop=False)
                    pe.matmul(bank, x_h, w_h, start=False, stop=False)
                    mm = pe.matmul(bank, x_l, w_h, start=False, stop=last and k == 1)
            mm.then_inc(slabs_used, 1)

        def norm_act(act, n, gain):
            act.activation(rstat[:, 5, :], rstat[:, 4, :], ACT.Ln, scale=1.0 / D, bias=rstat[:, 7, 0:1])\
               .then_inc(row_log, 1)
            act.wait_ge(row_log, n + 1)
            act.activation(rstat[:, 6, :], rstat[:, 5, :], ACT.Exp, scale=-0.5).then_inc(row_rstd, 1)
            for k in range(KD):
                act.wait_ge(turned, n * KD + k + 1)
                act.activation(hs[:, k, 0, :], ps[:, k % 8, 0:SEQ], ACT.Copy,
                               scale=par[:, gain + k:gain + k + 1]).then_inc(hi_made, 1)

        def norm_dve(dve, n, gain, src, dest):
            dve.wait_ge(row_rstd, n + 1)
            for t in range(TOK):
                dve.tensor_scalar(dest[:, t, :], src[:, t, :], rstat[:, 6, t:t + 1], None, ALU.mult)\
                   .then_inc(row_scaled, 1)
            for k in range(KD):
                dve.wait_ge(hi_made, n * KD + k + 1)
                dve.scalar_tensor_tensor(out=hs[:, k, 1, :],
                                         in0=ps[:, k % 8, 0:SEQ],
                                         scalar=par[:, gain + k:gain + k + 1], in1=hs[:, k, 0, :].bitcast(F32),
                                         op0=ALU.mult, op1=ALU.subtract).then_inc(lo_made, 1)

        def norm_pe(pe, n, scaled):
            pe.wait_ge(row_scaled, TOK * (n + 1))
            for k in range(KD):
                if k >= 8:
                    pe.wait_ge(lo_made, n * KD + k - 7)
                for t in range(TOK):
                    mm = pe.transpose(ps[:, k % 8, t * P:(t + 1) * P],
                                      scaled[:, t, k * P:(k + 1) * P], ident)
                mm.then_inc(turned, 1)

        @block.sync
        def _(sp):
            sp.dma_start(xt[:, :, :], x.rearrange("(t p) d -> p t d", p=P)).then_inc(x_loaded, 16)
            sp.dma_start(con[:, :], consts).then_inc(tables_loaded, 16)
            sp.dma_start(par[:, :], small).then_inc(tables_loaded, 16)
            sp.dma_start(wba[:, :, :], w_ba).then_inc(tables_loaded, 16)
            for s in range(SLOTS):
                sp.dma_start(raw[:, s], stream[s]).then_inc(raw_loaded[s], 16)
            with sp.Fori(1, TURNS) as turn:
                for s in range(SLOTS):
                    sp.wait_ge(lo_ready, turn * SLOTS + (s - SLOTS + 1))
                    sp.dma_start(raw[:, s], stream[bass.ds(turn * SLOTS + s, 1)].rearrange("o p n -> p (o n)"))\
                      .then_inc(raw_loaded[s], 16)
            sp.wait_ge(sg["y_stored"], 16 * 3 * TOK)
            sp.wait_ge(sg["last_stored"], 16 * TOK)

        @block.gpsimd
        def _(pool):
            pool.memset(ones[:, :], 1.0).then_inc(ones_set, 1)
            pool.wait_ge(gates_ready, 2)
            pool.memset(cin[:, :, 0:TAPS - 1], 0.0).then_inc(sg["c_zero"], 1)
            pool.wait_ge(sg["m_free"], HEADS + 1)
            pool.wait_ge(sg["c_sum"], 12)
            with pool.Fori(0, HEADS) as h:
                pool.wait_ge(sg["d_free"], h + 1)
                for j in range(2):
                    for t in range(TOK):
                        ins = pool.tensor_copy(d_cast[:, j, t, :], gcol[:, t, j, bass.ds(h, 1)].to_broadcast([P, P]))
                ins.then_inc(sg["d_cast_ready"], 1)
                pool.wait_ge(sg["d_exp"], h + 1)
                for t in range(TOK):
                    ins = pool.tensor_tensor(d_p[:, t, :], d_e[:, t, :], con[:, C_UP:C_UP + P], ALU.mult)
                ins.then_inc(sg["d_incl"], 1)
                pool.wait_ge(sg["d_amat"], h + 1)
                for j in range(LEVELS):
                    for t in range(TOK):
                        ins = pool.tensor_tensor(d_lv[:, j, t, :], d_vn[:, t, :],
                                                 con[:, C_LEVEL + j * P:C_LEVEL + (j + 1) * P], ALU.mult)
                    ins.then_inc(sg["d_levels"], 1)
                pool.wait_ge(sg["d_egrow"], h + 1)
                pool.tensor_tensor(d_qg[:, :], d_qg[:, :], d_qn[:, :], ALU.mult).then_inc(sg["d_qg_ready"], 1)
            pool.wait_ge(sg["g_merged"], 9)
            pool.dma_start(x1[:, :, :], x.rearrange("(t p) d -> p t d", p=P)).then_inc(x1_loaded, 16)
            for cb in range(3):
                for t in range(TOK):
                    if t == 0:
                        pool.wait_ge(sg["y_added"], cb + 1)
                    else:
                        read_out(pool, cb % 2, U_DWN + cb // 2)
                    pool.dma_start(out[t * P:(t + 1) * P, cb * 512:(cb + 1) * 512], x1[:, t, cb * 512:(cb + 1) * 512])\
                        .then_inc(sg["y_stored"], 16)

        @block.scalar
        def _(act):
            nc.scalar.preload_act_table_set("natural_log_exp_and_others")
            act.wait_ge(x_loaded, 16)
            for t in range(TOK):
                act.activation(hs[:, 4 * t:4 * t + 4, :, :].rearrange("p a b c -> p (a b c)"), xt[:, t, :], ACT.Square,
                               accum_out=rstat[:, 4, t:t + 1]).then_inc(row_sq, 1)
            act.wait_ge(tables_loaded, 48)
            act.activation(wbah[:, :, :], wba[:, :, :], ACT.Copy).then_inc(ba_hi, 1)
            act.wait_ge(row_sq, TOK + 1)
            norm_act(act, 0, S_ATTN)
            for n in range(AHEAD_HI):
                act.wait_ge(raw_loaded[n], 16)
                act.wait_ge(slabs_used, n + 1)
                act.activation(whi[:, n], raw[:, n], ACT.Copy).then_inc(hi_ready, 1)
            act.wait_ge(ba_done, 1)
            act.activation(gt[:, 1], ps[:, 6, 0:TOK * 2 * HEADS].rearrange("p (t j) -> p t j", t=TOK)[:, :, 0:HEADS],
                           ACT.Exp, scale=-1.0).then_inc(gate_a, 1)
            act.activation(gt[:, 4, 0, :], par[:, S_ALOG:S_ALOG + HEADS], ACT.Exp).then_inc(gate_a, 1)
            act.wait_ge(gate_v, 2)
            act.activation(gt[:, 3], gt[:, 2], ACT.Exp, scale=-1.0).then_inc(gate_a, 1)
            act.wait_ge(gate_a, 3)
            act.activation(gt[:, 2], gt[:, 3], ACT.Ln, bias=1.0).then_inc(gate_a, 1)
            act.wait_ge(gate_sums, 1)
            act.activation(glast[:, :, :], ps[:, 7, 64:64 + NCH * HEADS].rearrange("p (c h) -> p c h", c=NCH), ACT.Exp)
            act.activation(gcol[:, :, 2, :], ps[:, 7, 0:TOK * HEADS].rearrange("p (t h) -> p t h", t=TOK), ACT.Copy)\
               .then_inc(gate_a, 1)
            act.activation(gt[:, 5], ps[:, 7, 0:TOK * HEADS].rearrange("p (t h) -> p t h", t=TOK), ACT.Exp)\
               .then_inc(gate_a, 1)
            act.wait_ge(gate_v, 5)
            act.activation(gcol[:, :, 4, :], gt[:, 0], ACT.Exp).then_inc(gates_ready, 1)

            with act.Fori(0, 8) as it:
                for p in range(2):
                    for s in range(SLOTS):
                        cast(act, T_IN1 + it * 2 + p, s)
                        if s == 0 and p == 1:
                            copy_half(act, 0, T_IN1 + it * 2)
                copy_half(act, 1, T_IN1 + it * 2 + 1)

            def moba_reply(act, j, h):
                if j == 0:
                    act.wait_ge(sg["m_free"], h + 1)
                    act.activation(m_sq[:, 0, :], qkv[:, bass.ds(h, 1), :].rearrange("p o t -> p (o t)"), ACT.Square)
                    act.activation(m_sq[:, 1, :], qkv[:, bass.ds(h + HEADS, 1), :].rearrange("p o t -> p (o t)"),
                                   ACT.Square).then_inc(sg["m_squares"], 1)
                    act.activation(m_v[:, :], qkv[:, bass.ds(h + 2 * HEADS, 1), :].rearrange("p o t -> p (o t)"),
                                   ACT.Copy).then_inc(sg["m_v_ready"], 1)
                    act.wait_ge(sg["m_ssq"], h + 1)
                    act.activation(m_rs[:, :, :], ps[:, 6, :].rearrange("p (a t) -> p a t", a=2), ACT.Ln,
                                   scale=1.0 / HD, bias=rstat[:, 7, 0:1]).then_inc(sg["m_log"], 1)
                    act.wait_ge(sg["m_log"], h + 1)
                    act.activation(m_rs[:, :, :], m_rs[:, :, :], ACT.Exp, scale=-0.5).then_inc(sg["m_rstd"], 1)
                if j == 1:
                    act.wait_ge(sg["m_vturned"], h + 1)
                    act.activation(m_vt[:, :, :], ps[:, 6, 0:SEQ].rearrange("p (t d) -> p t d", t=TOK), ACT.Copy)\
                       .then_inc(sg["m_vt_ready"], 1)
                    act.wait_ge(sg["m_bias"], h + 1)
                    act.activation(m_s[:, 0:P], m_s[:, 0:P], ACT.Exp, scale=SCALE, bias=m_mx[:, 2:3],
                                   accum_out=m_mx[:, 4:5])
                    act.activation(m_s[:, P:3 * P], m_s[:, P:3 * P], ACT.Exp, scale=SCALE, bias=m_mx[:, 3:4],
                                   accum_out=m_mx[:, 5:6]).then_inc(sg["m_exp"], 1)
                if j == 2:
                    act.wait_ge(sg["m_pturned"], h + 1)
                    act.activation(m_pt[:, :], ps[:, 7, 0:3 * P], ACT.Copy).then_inc(sg["m_pt_ready"], 1)
                if j == 3:
                    act.wait_ge(sg["m_out"], h + 1)
                    act.activation(ya[:, bass.ds(h, 1), 0, :].rearrange("p o t -> p (o t)"), ps[:, 6, SEQ:2 * SEQ],
                                   ACT.Copy).then_inc(sg["m_hi"], 1)

            def conv_first_tap(act, it, g):
                read_out(act, g, it + (U_IN2 if g < 2 else 0))
                for c in range(2):
                    w = S_CONV + g * HEADS * TAPS
                    act.activation(cacc[:, c, :], cin[:, c, 0:SEQ], ACT.Copy,
                                   scale=par[:, bass.ds(w + (it * 2 + c) * TAPS, 1)]).then_inc(sg["c_tap"], 1)

            with act.Fori(0, 4) as it:
                for m in range(12):
                    cast(act, T_IN2 + it * 3 + m // 4, m % 4)
                    if m in (4, 8):
                        g = m // 4 - 1
                        copy_half(act, g, T_IN2 + it * 3 + g)
                        conv_first_tap(act, it, g)
                    for j in range(8):
                        if 6 * j // 4 == m:
                            moba_reply(act, j % 4, it * 2 + j // 4)
                copy_half(act, 2, T_IN2 + it * 3 + 2)
                conv_first_tap(act, it, 2)

            for q in range(4):
                if q == 0:
                    act.wait_ge(sg["c_sum"], 12)
                    act.wait_ge(sg["m_free"], HEADS + 1)
                part = dn[:, 2 * q:2 * q + 2]
                act.activation(part, part, ACT.Silu)
                part = z[:, 2 * q:2 * q + 2]
                ins = act.activation(part, part, ACT.Silu)
            ins.then_inc(sg["silu_done"], 1)
            act.wait_ge(sg["silu_done"], 1)
            nc.scalar.preload_act_table_set("natural_log_exp_and_others")

            with act.Fori(0, HEADS) as h:
                def step(m):
                    cast(act, T_IN3 + h * 2 + m // 4, m % 4)

                step(0)
                act.wait_ge(sg["d_free"], h + 1)
                act.activation(d_sq[:, :, :], dn[:, bass.ds(h, 1), 0:2, :].rearrange("p o a t -> p (o a) t"), ACT.Square)\
                   .then_inc(sg["d_squares"], 1)
                act.activation(d_v[:, :], dn[:, bass.ds(h, 1), 2, :].rearrange("p o t -> p (o t)"), ACT.Copy)\
                   .then_inc(sg["d_v_ready"], 1)
                act.wait_ge(sg["d_ssq"], h + 1)
                act.activation(d_sq[:, :, :], ps[:, 4, :].rearrange("p (a t) -> p a t", a=2), ACT.Ln,
                               bias=rstat[:, 7, 0:1]).then_inc(sg["d_log"], 1)
                act.wait_ge(sg["d_log"], h + 1)
                act.activation(d_sq[:, :, :], d_sq[:, :, :], ACT.Exp, scale=-0.5).then_inc(sg["d_rstd"], 1)
                act.wait_ge(sg["d_rows"], h + 1)
                act.activation(d_qg[:, :], ps[:, 5, 0:SEQ], ACT.Exp).then_inc(sg["d_egrow"], 1)
                act.wait_ge(sg["d_arg"], h + 1)
                act.activation(d_e[:, :, :], d_e[:, :, :], ACT.Exp).then_inc(sg["d_exp"], 1)
                step(1)
                act.wait_ge(sg["d_tok"], h + 1)
                for t in range(TOK):
                    act.activation(d_vb[:, t, :], ps[:, 6, SEQ + t * P:SEQ + (t + 1) * P], ACT.Copy,
                                   scale=gcol[:, t, 1, bass.ds(h, 1)]).then_inc(sg["d_vb_ready"], 1)
                for t in range(TOK):
                    act.activation(d_kbg[:, t, :], ps[:, 6, t * P:(t + 1) * P], ACT.Copy,
                                   scale=gcol[:, t, 3, bass.ds(h, 1)]).then_inc(sg["d_kbg_ready"], 1)
                for j in range(1, LEVELS):
                    act.wait_ge(sg["d_p_done"], h * (LEVELS - 1) + j)
                    act.activation(d_p[:, :, :], ps[:, 4, 0:SEQ].rearrange("p (t d) -> p t d", t=TOK), ACT.Copy)\
                       .then_inc(sg["d_p_ready"], 1)
                    if j in (1, 2, 4, 5):
                        step({1: 2, 2: 3, 4: 4, 5: 5}[j])
                copy_half(act, 0, T_IN3 + h * 2)
                act.wait_ge(sg["d_uw"], h + 1)
                act.activation(d_uw[:, :, :, :], ps[:, 7, :].rearrange("p (a t d) -> p a t d", a=2, t=TOK), ACT.Copy)\
                   .then_inc(sg["d_u_ready"], 1)
                step(6)
                step(7)
                act.wait_ge(sg["d_okv"], h * NCH + NCH)
                act.activation(d_sq[:, 0, :], ps[:, 6, 0:SEQ], ACT.Square).then_inc(sg["d_osq"], 1)
                act.wait_ge(sg["d_ossq"], h + 1)
                act.activation(d_sq[:, 1, :], ps[:, 7, 0:SEQ], ACT.Ln, scale=1.0 / HD, bias=rstat[:, 7, 0:1])\
                   .then_inc(sg["d_olog"], 1)
                act.wait_ge(sg["d_olog"], h + 1)
                act.activation(d_sq[:, 1, :], d_sq[:, 1, :], ACT.Exp, scale=-0.5).then_inc(sg["d_orstd"], 1)
                act.wait_ge(sg["d_y"], h + 1)
                copy_half(act, 1, T_IN3 + h * 2 + 1)
                act.activation(yb[:, bass.ds(h, 1), 0, :].rearrange("p o t -> p (o t)"), d_kb[:, :], ACT.Copy)\
                   .then_inc(sg["d_yhi"], 1)

            read_out(act, 1, U_MRG - 1)
            nc.scalar.preload_act_table_set("sigmoid_and_others")
            with act.Fori(0, 8) as g:
                sig = mg[:, 0:2, :].rearrange("p a (b t) -> p (a b) t", t=SEQ)

                def gate(j):
                    if j == 0:
                        act.wait_ge(sg["g_merged"], g + 1)
                    act.activation(sig[:, 2 * j:2 * j + 2], gates[:, bass.ds(g * 2 + j * KD, 2), :], ACT.Sigmoid)\
                       .then_inc(sg["g_sig"], 1)
                for s in range(SLOTS):
                    cast(act, T_MRG + g, s)
                    if s == 0:
                        gate(0)
                    if s == 1:
                        gate(1)
                    if s == 2:
                        copy_half(act, 0, T_MRG + g, 1)
                copy_half(act, 1, T_MRG + g)
                act.wait_ge(sg["merged"], g + 1)
                act.activation(hs[:, bass.ds(g * 2, 2), 0, :], mg[:, 2, :].rearrange("p (b t) -> p b t", t=SEQ), ACT.Copy)\
                   .then_inc(sg["g_hi"], 1)

            nc.scalar.preload_act_table_set("natural_log_exp_and_others")

            def new_squares(act, p, it):
                for t in range(TOK):
                    if t == 0:
                        act.wait_ge(sg["x1_added"], it * 2 + p + 1)
                    else:
                        read_out(act, p, U_OUT + it)
                    act.wait_ge(sg["x1_sq"], it * 4 + p * TOK + t + 1)
                    act.activation(half[:, 0].rearrange("p a t -> p (a t)"), x1[:, t, bass.ds(it * 1024 + p * 512, 512)],
                                   ACT.Square, accum_out=rstat[:, bass.ds(it * 2 + p, 1), t]).then_inc(sg["x1_sq"], 1)
            with act.Fori(0, 2) as it:
                for p in range(2):
                    for s in range(8):
                        cast(act, T_OUT + it * 4 + p * 2 + s // 4, s % 4)
                        if p == 1 and s == 2:
                            new_squares(act, 0, it)
                new_squares(act, 1, it)
            act.wait_ge(sg["stat_sum"], 1)
            norm_act(act, 1, S_FFN)

            nc.scalar.preload_act_table_set("silu_and_others")
            with act.Fori(0, 22) as g:
                for m in range(8):
                    cast(act, T_FFN + g * 2 + m // 4, m % 4)
                    if m == 4:
                        copy_half(act, 0, T_FFN + g * 2)
                        read_out(act, 0, U_FFN + g)
                        for c in range(2):
                            act.activation(facc[:, c, :], fin[:, c, 0:SEQ], ACT.Identity,
                                           scale=par[:, bass.ds(S_FCONV + (g * 2 + c) * FTAPS, 1)],
                                           bias=par[:, bass.ds(S_FBIAS + g * 2 + c, 1)]).then_inc(sg["f_tap"], 1)
                    if m == 5:
                        act.wait_ge(sg["f_acc"], (g + 1) * 4)
                        act.activation(facc[:, :, :], facc[:, :, :], ACT.Silu).then_inc(sg["f_silu"], 1)
                copy_half(act, 1, T_FFN + g * 2 + 1)
                act.wait_ge(sg["f_prod"], g + 1)
                act.activation(act_s[:, bass.ds(g * 2, 2), 0, :], facc[:, :, :], ACT.Copy).then_inc(sg["f_hi"], 1)

            with act.Fori(0, 21) as turn:
                for s in range(SLOTS):
                    cast(act, T_DWN + turn, s)
            cast(act, T_DWN + 21, 0)
            for t in range(TOK):
                if t == 0:
                    act.wait_ge(sg["y_added"], 4)
                else:
                    read_out(act, 1, U_DWN + 1)
                act.dma_start(out[t * P:(t + 1) * P, 3 * 512:4 * 512], x1[:, t, 3 * 512:4 * 512])\
                   .then_inc(sg["last_stored"], 16)

        @block.vector
        def _(dve):
            dve.memset(rstat[:, 7, :], EPS).then_inc(row_sq, 1)
            dve.sem_inc(slabs_used, SLOTS)
            for p in range(3):
                dve.sem_inc(pair_free[p], 1)
            dve.sem_inc(sg["m_free"], 1)
            dve.sem_inc(sg["d_free"], 1)
            dve.sem_inc(sg["g_merged"], 1)
            dve.sem_inc(sg["x1_sq"], 1)
            dve.wait_ge(ba_hi, 1)
            dve.tensor_tensor(wbal[:, :, :], wba[:, :, :], wbah[:, :, :].bitcast(F32), ALU.subtract).then_inc(ba_lo, 1)
            norm_dve(dve, 0, S_ATTN, xt, xt)
            for n in range(AHEAD_LO):
                dve.wait_ge(hi_ready, n + 1)
                dve.tensor_tensor(wlo[:, n], raw[:, n], whi[:, n].bitcast(F32), ALU.subtract).then_inc(lo_ready, 1)
            dve.wait_ge(gate_a, 1)
            a_in = ps[:, 6, 0:TOK * 2 * HEADS].rearrange("p (t j) -> p t j", t=TOK)[:, :, HEADS:2 * HEADS]
            for t in range(TOK):
                ins = dve.tensor_tensor(gt[:, 0, t, :], a_in[:, t, :], par[:, S_DT:S_DT + HEADS], ALU.add)
            ins.then_inc(gate_v, 1)
            dve.wait_ge(gate_v, 1)
            dve.scalar_tensor_tensor(out=gt[:, 2], in0=gt[:, 0], scalar=-1.0, in1=gt[:, 0], op0=ALU.mult, op1=ALU.max)\
               .then_inc(gate_v, 1)
            dve.wait_ge(gate_a, 4)
            dve.tensor_scalar(gt[:, 1], gt[:, 1], 1.0, None, ALU.add)
            dve.scalar_tensor_tensor(out=gt[:, 5], in0=gt[:, 0], scalar=0.0, in1=gt[:, 2], op0=ALU.max, op1=ALU.add)\
               .then_inc(gate_v, 1)
            dve.wait_ge(gate_v, 3)
            dve.reciprocal(gcol[:, :, 1, :], gt[:, 1])
            for t in range(TOK):
                ins = dve.scalar_tensor_tensor(out=gcol[:, t, 0, :], in0=gt[:, 5, t, :], scalar=-1.0,
                                               in1=gt[:, 4, 0, :], op0=ALU.mult, op1=ALU.mult)
            ins.then_inc(gate_v, 1)
            dve.wait_ge(gate_a, 6)
            dve.tensor_tensor(gt[:, 0], ps[:, 7, 32:32 + TOK * HEADS].rearrange("p (t h) -> p t h", t=TOK),
                              gcol[:, :, 2, :], ALU.subtract).then_inc(gate_v, 1)
            dve.tensor_tensor(gcol[:, :, 3, :], gt[:, 5], gcol[:, :, 1, :], ALU.mult).then_inc(gates_ready, 1)

            def in1_loop(count, first, dest):
                with dve.Fori(0, count) as it:
                    for p in range(2):
                        for s in range(SLOTS):
                            split(dve, T_IN1 + (it + first) * 2 + p, s)
                            if s == 0 and p == 1:
                                add_halves(dve, 0, U_IN1 + first + it, dest[:, bass.ds(it * 4, 2), :])
                    add_halves(dve, 1, U_IN1 + first + it, dest[:, bass.ds(it * 4 + 2, 2), :])
            in1_loop(6, 0, qkv)
            in1_loop(2, 6, z)

            def moba_reply(dve, j, h):
                if j == 0:
                    dve.wait_ge(sg["m_rstd"], h + 1)
                    dve.scalar_tensor_tensor(out=m_qn[:, :], in0=qkv[:, bass.ds(h, 1), :].rearrange("p o t -> p (o t)"),
                                             scalar=par[:, S_QG:S_QG + 1], in1=m_rs[:, 0, :], op0=ALU.mult,
                                             op1=ALU.mult)
                    dve.scalar_tensor_tensor(out=m_kn[:, :],
                                             in0=qkv[:, bass.ds(h + HEADS, 1), :].rearrange("p o t -> p (o t)"),
                                             scalar=par[:, S_KG:S_KG + 1], in1=m_rs[:, 1, :], op0=ALU.mult,
                                             op1=ALU.mult).then_inc(sg["m_qn_ready"], 1)
                if j == 1:
                    dve.wait_ge(sg["m_scores"], h + 1)
                    dve.tensor_tensor(m_s[:, :], ps[:, 7, 0:3 * P], con[:, C_CAUSAL:C_CAUSAL + 3 * P], ALU.add)\
                       .then_inc(sg["m_masked"], 1)
                    dve.wait_ge(sg["m_masked"], h + 1)
                    dve.reduce_max(m_mx[:, 0:1], m_s[:, 0:P], AX_X)
                    dve.reduce_max(m_mx[:, 1:2], m_s[:, P:3 * P], AX_X).then_inc(sg["m_max"], 1)
                    dve.wait_ge(sg["m_max"], h + 1)
                    dve.tensor_scalar(m_mx[:, 2:4], m_mx[:, 0:2], -SCALE, None, ALU.mult).then_inc(sg["m_bias"], 1)
                    dve.wait_ge(sg["m_exp"], h + 1)
                    dve.reciprocal(m_mx[:, 6:8], m_mx[:, 4:6]).then_inc(sg["m_rinv"], 1)
                    dve.wait_ge(sg["m_rinv"], h + 1)
                    dve.tensor_scalar(m_s[:, 0:P], m_s[:, 0:P], m_mx[:, 6:7], None, ALU.mult)
                    dve.tensor_scalar(m_s[:, P:3 * P], m_s[:, P:3 * P], m_mx[:, 7:8], None, ALU.mult)\
                       .then_inc(sg["m_prob"], 1)
                if j == 3:
                    dve.wait_ge(sg["m_hi"], h + 1)
                    dve.tensor_tensor(ya[:, bass.ds(h, 1), 1, :].rearrange("p o t -> p (o t)"), ps[:, 6, SEQ:2 * SEQ],
                                      ya[:, bass.ds(h, 1), 0, :].rearrange("p o t -> p (o t)").bitcast(F32),
                                      ALU.subtract).then_inc(sg["m_free"], 1)

            def conv(dve, it, g, p, use):
                add_halves(dve, p, use, cin[:, :, TAPS - 1:TAPS - 1 + SEQ])
                w = S_CONV + g * HEADS * TAPS
                for tap in range(1, TAPS):
                    for c in range(2):
                        if tap == 1:
                            read_out(dve, p, use)
                            dve.wait_ge(sg["c_tap"], (it * 3 + g) * 2 + c + 1)
                        else:
                            dve.wait_ge(sg["c_acc"], (it * 3 + g) * 4 + tap * 2 + c - 3)
                        last = tap == TAPS - 1
                        dest = dn[:, bass.ds(it * 2 + c, 1), g, :].rearrange("p o t -> p (o t)") if last \
                            else cacc[:, c, :]
                        ins = dve.scalar_tensor_tensor(out=dest, in0=cin[:, c, tap:tap + SEQ],
                                                       scalar=par[:, bass.ds(w + (it * 2 + c) * TAPS + tap, 1)],
                                                       in1=cacc[:, c, :], op0=ALU.mult, op1=ALU.add)
                        if not last:
                            ins.then_inc(sg["c_acc"], 1)
                ins.then_inc(sg["c_sum"], 1)

            read_out(dve, 1, U_IN2 - 1)
            dve.wait_ge(sg["c_zero"], 1)
            with dve.Fori(0, 4) as it:
                for m in range(12):
                    split(dve, T_IN2 + it * 3 + m // 4, m % 4)
                    if m in (4, 8):
                        conv(dve, it, m // 4 - 1, m // 4 - 1, it + U_IN2)
                    for j in range(8):
                        if 6 * j // 4 == m:
                            moba_reply(dve, j % 4, it * 2 + j // 4)
                conv(dve, it, 2, 2, it)

            with dve.Fori(0, HEADS) as h:
                def step(m):
                    split(dve, T_IN3 + h * 2 + m // 4, m % 4)

                step(0)
                dve.wait_ge(sg["silu_done"], 1)
                dve.wait_ge(sg["d_rstd"], h + 1)
                dve.scalar_tensor_tensor(out=d_qn[:, :], in0=dn[:, bass.ds(h, 1), 0, :].rearrange("p o t -> p (o t)"),
                                         scalar=SCALE, in1=d_sq[:, 0, :], op0=ALU.mult, op1=ALU.mult)
                dve.tensor_tensor(d_kn[:, :], dn[:, bass.ds(h, 1), 1, :].rearrange("p o t -> p (o t)"), d_sq[:, 1, :],
                                  ALU.mult).then_inc(sg["d_norm"], 1)
                dve.wait_ge(sg["d_egrow"], h + 1)
                for t in range(TOK):
                    ins = dve.tensor_scalar(d_e[:, t, :], ps[:, 5, t * P:(t + 1) * P], gcol[:, t, 2, bass.ds(h, 1)], 0.0,
                                            ALU.subtract, ALU.min)
                ins.then_inc(sg["d_arg"], 1)
                dve.wait_ge(sg["d_norm"], h + 1)
                dve.tensor_tensor(d_kb[:, :], d_kn[:, :], ps[:, 5, SEQ:2 * SEQ], ALU.mult).then_inc(sg["d_kb_ready"], 1)
                step(1)
                dve.wait_ge(sg["d_prod"], h + 1)
                dve.wait_ge(sg["d_exp"], h + 1)
                dve.tensor_tensor(d_vn[:, :, :], ps[:, 7, 0:SEQ].rearrange("p (t d) -> p t d", t=TOK), d_e[:, :, :],
                                  ALU.mult).then_inc(sg["d_amat"], 1)
                dve.wait_ge(sg["d_incl"], h + 1)
                dve.tensor_tensor(d_at[:, :, :], ps[:, 7, SEQ:2 * SEQ].rearrange("p (t d) -> p t d", t=TOK),
                                  d_p[:, :, :], ALU.mult).then_inc(sg["d_attn"], 1)
                dve.wait_ge(sg["d_levels"], h * LEVELS + 1)
                for t in range(TOK):
                    ins = dve.tensor_tensor(d_tu[:, 1, t, :], ident, d_lv[:, 0, t, :], ALU.subtract)
                dve.wait_ge(sg["d_l0"], h + 1)
                for t in range(TOK):
                    ins = dve.tensor_tensor(d_tu[:, 0, t, :], ident, ps[:, 4, t * P:(t + 1) * P], ALU.subtract)
                ins.then_inc(sg["d_tu_ready"], 1)
                for j in range(1, LEVELS):
                    first = 0 if j < LEVELS - 1 else 1
                    dve.wait_ge(sg["d_tu_done"], h * (LEVELS - 1) + j)
                    dve.tensor_tensor(d_tu[:, first:2], d_tu[:, first:2],
                                      ps[:, 5, first * SEQ:].rearrange("p (a t d) -> p a t d", t=TOK, d=P),
                                      ALU.subtract).then_inc(sg["d_tu_ready"], 1)
                    if j in (1, 2, 4, 5):
                        step({1: 2, 2: 3, 4: 4, 5: 5}[j])
                dve.wait_ge(sg["d_kbg_ready"], (h + 1) * TOK)
                for t in range(TOK):
                    ins = dve.tensor_scalar(d_kd[:, t, :], ps[:, 6, t * P:(t + 1) * P], gcol[:, t, 4, bass.ds(h, 1)],
                                            None, ALU.mult)
                ins.then_inc(sg["d_kd_ready"], 1)
                add_halves(dve, 0, U_IN3 + h, gates[:, bass.ds(h * 4, 2), :])
                dve.wait_ge(sg["d_u_ready"], h + 1)
                dve.wait_ge(sg["d_levels"], (h + 1) * LEVELS)
                for c in range(NCH):
                    t, o = c // 2, (c % 2) * CHUNK
                    if c == 0:
                        dve.tensor_copy(d_vn[o:o + CHUNK, t, :], d_uw[o:o + CHUNK, 0, t, :]).then_inc(sg["d_vn_ready"], 1)
                    else:
                        dve.wait_ge(sg["d_ws"], h * (NCH - 1) + c)
                        dve.tensor_tensor(d_vn[o:o + CHUNK, t, :], d_uw[o:o + CHUNK, 0, t, :], ps[o:o + CHUNK, 4, 0:P],
                                          ALU.subtract).then_inc(sg["d_vn_ready"], 1)
                    dve.wait_ge(sg["d_okv"], h * NCH + c + 1)
                    if c == 0:
                        dve.tensor_copy(d_state[:, :], ps[:, 5, 0:P]).then_inc(sg["d_state_ready"], 1)
                    elif c < NCH - 1:
                        dve.scalar_tensor_tensor(out=d_state[:, :], in0=d_state[:, :],
                                                 scalar=glast[:, c, bass.ds(h, 1)], in1=ps[:, 5, 0:P], op0=ALU.mult,
                                                 op1=ALU.add).then_inc(sg["d_state_ready"], 1)
                    if c in (1, 2):
                        step(5 + c)
                dve.wait_ge(sg["d_orstd"], h + 1)
                dve.scalar_tensor_tensor(out=d_kn[:, :], in0=ps[:, 6, 0:SEQ], scalar=par[:, S_OG:S_OG + 1],
                                         in1=d_sq[:, 1, :], op0=ALU.mult, op1=ALU.mult).then_inc(sg["d_on"], 1)
                dve.wait_ge(sg["d_on"], h + 1)
                dve.tensor_tensor(d_kb[:, :], d_kn[:, :], z[:, bass.ds(h, 1), :].rearrange("p o t -> p (o t)"), ALU.mult)\
                   .then_inc(sg["d_y"], 1)
                dve.wait_ge(sg["d_yhi"], h + 1)
                dve.tensor_tensor(yb[:, bass.ds(h, 1), 1, :].rearrange("p o t -> p (o t)"), d_kb[:, :],
                                  yb[:, bass.ds(h, 1), 0, :].rearrange("p o t -> p (o t)").bitcast(F32), ALU.subtract)\
                   .then_inc(sg["d_free"], 1)
                add_halves(dve, 1, U_IN3 + h, gates[:, bass.ds(h * 4 + 2, 2), :])

            with dve.Fori(0, 8) as g:
                sig = mg[:, 0:2, :].rearrange("p a (b t) -> p a b t", t=SEQ)
                prod = mg[:, 2:4, :].rearrange("p a (b t) -> p a b t", t=SEQ)

                def branch(j):
                    add_halves(dve, j, U_MRG + g, prod[:, j])
                    read_out(dve, j, U_MRG + g)
                    dve.wait_ge(sg["g_sig"], g * 2 + j + 1)
                    dve.tensor_tensor(prod[:, j], prod[:, j], sig[:, j], ALU.mult).then_inc(sg["g_mul"], 1)
                for s in range(SLOTS):
                    split(dve, T_MRG + g, s)
                    if s == 2:
                        branch(0)
                branch(1)
                dve.wait_ge(sg["g_mul"], g * 2 + 2)
                dve.tensor_tensor(prod[:, 0], prod[:, 0], prod[:, 1], ALU.add).then_inc(sg["merged"], 1)
                dve.wait_ge(sg["g_hi"], g + 1)
                dve.tensor_tensor(hs[:, bass.ds(g * 2, 2), 1, :], prod[:, 0], hs[:, bass.ds(g * 2, 2), 0, :].bitcast(F32),
                                  ALU.subtract).then_inc(sg["g_merged"], 1)

            dve.wait_ge(x1_loaded, 16)

            def residual(p, turn, s, col, done):
                multiplied(dve, turn, s)
                for t, signal in enumerate((done, pair_free[p])):
                    part = x1[:, t, bass.ds(col, 512)]
                    dve.tensor_tensor(part, part, ps[:, 2 * p + t, :], ALU.add).then_inc(signal, 1)
            with dve.Fori(0, 2) as it:
                for p in range(2):
                    for s in range(8):
                        split(dve, T_OUT + it * 4 + p * 2 + s // 4, s % 4)
                        if p == 1 and s == 2:
                            residual(0, T_OUT + it * 4 + 1, 3, it * 1024, sg["x1_added"])
                residual(1, T_OUT + it * 4 + 3, 3, it * 1024 + 512, sg["x1_added"])
            dve.wait_ge(sg["x1_sq"], 9)
            dve.reduce_sum(rstat[:, 4, :], rstat[:, 0:4, :].rearrange("p a t -> p t a"), AX_X)\
               .then_inc(sg["stat_sum"], 1)
            norm_dve(dve, 1, S_FFN, x1, scaled)

            dve.memset(fin[:, :, 0:FTAPS - 1], 0.0).then_inc(sg["f_zero"], 1)
            with dve.Fori(0, 22) as g:
                for m in range(8):
                    split(dve, T_FFN + g * 2 + m // 4, m % 4)
                    if m == 4:
                        add_halves(dve, 0, U_FFN + g, fin[:, :, FTAPS - 1:FTAPS - 1 + SEQ], U_FFN - U_OUT)
                        for tap in range(1, FTAPS):
                            for c in range(2):
                                if tap == 1:
                                    read_out(dve, 0, U_FFN + g)
                                    dve.wait_ge(sg["f_tap"], g * 2 + c + 1)
                                else:
                                    dve.wait_ge(sg["f_acc"], g * 4 + c + 1)
                                dve.scalar_tensor_tensor(
                                    out=facc[:, c, :], in0=fin[:, c, tap:tap + SEQ],
                                    scalar=par[:, bass.ds(S_FCONV + (g * 2 + c) * FTAPS + tap, 1)],
                                    in1=facc[:, c, :], op0=ALU.mult, op1=ALU.add).then_inc(sg["f_acc"], 1)
                fup = fin[:, :, FTAPS - 1:FTAPS - 1 + SEQ]
                add_halves(dve, 1, U_FFN + g, fup, U_FFN - U_OUT)
                read_out(dve, 1, U_FFN + g)
                dve.wait_ge(sg["f_silu"], g + 1)
                dve.tensor_tensor(facc[:, :, :], facc[:, :, :], fup, ALU.mult).then_inc(sg["f_prod"], 1)
                dve.wait_ge(sg["f_hi"], g + 1)
                dve.tensor_tensor(act_s[:, bass.ds(g * 2, 2), 1, :], facc[:, :, :],
                                  act_s[:, bass.ds(g * 2, 2), 0, :].bitcast(F32), ALU.subtract)\
                   .then_inc(sg["hidden_ready"], 1)

            for cb in range(4):
                for j in range(22):
                    n = cb * 22 + j
                    if n < 88 - AHEAD_LO:
                        split(dve, T_DWN + n // 4, n % 4)
                    if j == 4 and cb > 0:
                        last = cb * 22 - 1
                        residual((cb - 1) % 2, T_DWN + last // 4, last % 4, (cb - 1) * 512, sg["y_added"])
            residual(1, TURNS - 1, 3, 3 * 512, sg["y_added"])

        @block.tensor
        def _(pe):
            pe.wait_ge(tables_loaded, 48)
            norm_pe(pe, 0, xt)
            pe.wait_ge(lo_made, KD)
            pe.wait_ge(ba_lo, 1)
            for t in range(TOK):
                for k in range(KD):
                    x_h, x_l = hs[:, k, 0, t * P:(t + 1) * P], hs[:, k, 1, t * P:(t + 1) * P]
                    dst = ps[:, 6, t * 2 * HEADS:(t + 1) * 2 * HEADS]
                    pe.matmul(dst, x_h, wbal[:, k, :], start=k == 0, stop=False)
                    pe.matmul(dst, x_h, wbah[:, k, :], start=False, stop=False)
                    mm = pe.matmul(dst, x_l, wbah[:, k, :], start=False, stop=k == KD - 1)
            mm.then_inc(ba_done, 1)
            pe.wait_ge(gate_v, 4)
            pe.wait_ge(ones_set, 1)
            same, up = con[:, C_SAME:C_SAME + P], con[:, C_UP:C_UP + P]
            for t in range(TOK):
                g_t = gcol[:, t, 0, :]
                pe.matmul(ps[:, 7, t * HEADS:(t + 1) * HEADS], up, g_t, start=True, stop=True)
                pe.matmul(ps[:, 7, 32 + t * HEADS:32 + (t + 1) * HEADS], same, g_t, start=True, stop=True)
                for o in range(2):
                    c = 2 * t + o
                    mm = pe.matmul(ps[:, 7, 64 + c * HEADS:64 + (c + 1) * HEADS],
                                   con[:, C_HALF + o * P:C_HALF + (o + 1) * P], g_t, start=True, stop=True)
            mm.then_inc(gate_sums, 1)

            with pe.Fori(0, 8) as it:
                for p in range(2):
                    channel_group(pe, T_IN1 + it * 2 + p, p, U_IN1 + it, hs)

            def moba_step(pe, j, h):
                if j == 0:
                    pe.wait_ge(sg["m_squares"], h + 1)
                    pe.matmul(ps[:, 6, :], ones[:, :], m_sq[:, :, :].rearrange("p a t -> p (a t)"), start=True,
                              stop=True).then_inc(sg["m_ssq"], 1)
                if j == 1:
                    pe.wait_ge(sg["m_qn_ready"], h + 1)
                    pe.matmul(ps[:, 7, 0:P], m_qn[:, 0:P], m_kn[:, 0:P], start=True, stop=True)
                    pe.matmul(ps[:, 7, P:3 * P], m_qn[:, P:2 * P], m_kn[:, :], start=True, stop=True)\
                      .then_inc(sg["m_scores"], 1)
                    pe.wait_ge(sg["m_v_ready"], h + 1)
                    for t in range(TOK):
                        mm = pe.transpose(ps[:, 6, t * P:(t + 1) * P], m_v[:, t * P:(t + 1) * P], ident)
                    mm.then_inc(sg["m_vturned"], 1)
                if j == 2:
                    pe.wait_ge(sg["m_prob"], h + 1)
                    for i in range(3):
                        mm = pe.transpose(ps[:, 7, i * P:(i + 1) * P], m_s[:, i * P:(i + 1) * P], ident)
                    mm.then_inc(sg["m_pturned"], 1)
                if j == 3:
                    pe.wait_ge(sg["m_pt_ready"], h + 1)
                    pe.wait_ge(sg["m_vt_ready"], h + 1)
                    pe.matmul(ps[:, 6, SEQ:SEQ + P], m_vt[:, 0, :], m_pt[:, 0:P], start=True, stop=True)
                    pe.matmul(ps[:, 6, SEQ + P:2 * SEQ], m_vt[:, 0, :], m_pt[:, P:2 * P], start=True, stop=False)
                    pe.matmul(ps[:, 6, SEQ + P:2 * SEQ], m_vt[:, 1, :], m_pt[:, 2 * P:3 * P], start=False,
                              stop=True).then_inc(sg["m_out"], 1)

            pe.wait_ge(gates_ready, 2)
            with pe.Fori(0, 4) as it:
                for i in range(48):
                    if i % 6 == 0:
                        moba_step(pe, i // 6 % 4, it * 2 + i // 24)
                    g = i // 16
                    channel_unit(pe, T_IN2 + it * 3 + g, i // 4 % 4, i % 4, g, it + (U_IN2 if g < 2 else 0), hs, i % 16,
                                 i % 16 == 0, i % 16 == 15)

            pe.wait_ge(pair_free[2], 5)
            pe.wait_ge(sg["m_free"], HEADS + 1)
            with pe.Fori(0, HEADS) as h:
                def fill(step):
                    for i in range(step * 4 // 3, (step + 1) * 4 // 3):
                        g = i // 16
                        channel_unit(pe, T_IN3 + h * 2 + g, i // 4 % 4, i % 4, g, U_IN3 + h, hs, i % 16, i % 16 == 0,
                                     i % 16 == 15)

                def both(out, lhs, rhs, col=0):
                    for t in range(TOK):
                        mm = pe.matmul(ps[:, out, col + t * P:col + (t + 1) * P], lhs(t), rhs(t), start=True, stop=True)
                    return mm

                pe.wait_ge(sg["d_squares"], h + 1)
                pe.matmul(ps[:, 4, :], ones[:, :], d_sq[:, :, :].rearrange("p a t -> p (a t)"), start=True, stop=True)\
                  .then_inc(sg["d_ssq"], 1)
                fill(0)
                pe.wait_ge(sg["d_cast_ready"], h + 1)
                both(5, lambda t: d_cast[:, 0, t, :], lambda t: up)
                both(5, lambda t: d_cast[:, 1, t, :], lambda t: ident, SEQ).then_inc(sg["d_rows"], 1)
                fill(1)
                pe.wait_ge(sg["d_norm"], h + 1)
                pe.wait_ge(sg["d_v_ready"], h + 1)
                for t in range(TOK):
                    pe.transpose(ps[:, 6, t * P:(t + 1) * P], d_kn[:, t * P:(t + 1) * P], ident)
                    mm = pe.transpose(ps[:, 6, SEQ + t * P:SEQ + (t + 1) * P], d_v[:, t * P:(t + 1) * P], ident)
                mm.then_inc(sg["d_tok"], 1)
                fill(2)
                pe.wait_ge(sg["d_kb_ready"], h + 1)
                both(7, lambda t: d_kn[:, t * P:(t + 1) * P], lambda t: d_kb[:, t * P:(t + 1) * P])
                both(7, lambda t: d_kn[:, t * P:(t + 1) * P], lambda t: d_qn[:, t * P:(t + 1) * P], SEQ)\
                    .then_inc(sg["d_prod"], 1)
                fill(3)
                pe.wait_ge(sg["d_levels"], h * LEVELS + 1)
                both(4, lambda t: d_lv[:, 0, t, :], lambda t: ident).then_inc(sg["d_l0"], 1)
                fill(4)
                for j in range(1, LEVELS):
                    pe.wait_ge(sg["d_levels"], h * LEVELS + j + 1)
                    pe.wait_ge(sg["d_tu_ready"], h * LEVELS + j)
                    if j == 1:
                        pe.wait_ge(sg["d_attn"], h + 1)
                    both(4, lambda t: d_lv[:, j, t, :], lambda t: d_tu[:, 0, t, :]).then_inc(sg["d_p_done"], 1)
                    fill(3 + 2 * j)
                    pe.wait_ge(sg["d_p_ready"], h * (LEVELS - 1) + j)
                    if j == 1:
                        pe.wait_ge(sg["d_egrow"], h + 1)
                    if j < LEVELS - 1:
                        both(5, lambda t: d_tu[:, 1, t, :], lambda t: d_p[:, t, :])
                    both(5, lambda t: d_p[:, t, :], lambda t: d_tu[:, 1, t, :], SEQ).then_inc(sg["d_tu_done"], 1)
                    fill(4 + 2 * j)
                pe.wait_ge(sg["d_tu_ready"], (h + 1) * LEVELS)
                pe.wait_ge(sg["d_vb_ready"], (h + 1) * TOK)
                pe.wait_ge(sg["d_kbg_ready"], (h + 1) * TOK)
                both(7, lambda t: d_tu[:, 1, t, :], lambda t: d_vb[:, t, :])
                both(7, lambda t: d_kbg[:, t, :], lambda t: d_tu[:, 1, t, :], SEQ).then_inc(sg["d_uw"], 1)
                fill(15)
                pe.wait_ge(sg["d_u_ready"], h + 1)
                pe.wait_ge(sg["d_qg_ready"], h + 1)
                pe.wait_ge(sg["d_kd_ready"], h + 1)
                for c in range(NCH):
                    t, o = c // 2, (c % 2) * CHUNK
                    if c > 0:
                        pe.wait_ge(sg["d_state_ready"], h * (NCH - 1) + c)
                        pe.matmul(ps[o:o + CHUNK, 4, 0:P], d_uw[:, 1, t, o:o + CHUNK], d_state[:, :], start=True,
                                  stop=True).then_inc(sg["d_ws"], 1)
                        fill(15 + 2 * c)
                    pe.wait_ge(sg["d_vn_ready"], h * NCH + c + 1)
                    dst = ps[:, 6, c * CHUNK:(c + 1) * CHUNK]
                    if c > 0:
                        pe.matmul(dst, d_state[:, :], d_qg[:, c * CHUNK:(c + 1) * CHUNK], start=True, stop=False)
                    mm = pe.matmul(dst, d_vn[o:o + CHUNK, t, :], d_at[o:o + CHUNK, t, o:o + CHUNK], start=c == 0,
                                   stop=True)
                    if c < NCH - 1:
                        mm = pe.matmul(ps[:, 5, 0:P], d_kd[o:o + CHUNK, t, :], d_vn[o:o + CHUNK, t, :], start=True,
                                       stop=True)
                    mm.then_inc(sg["d_okv"], 1)
                    fill(16 + 2 * c)
                pe.wait_ge(sg["d_osq"], h + 1)
                pe.matmul(ps[:, 7, 0:SEQ], ones[:, :], d_sq[:, 0, :], start=True, stop=True).then_inc(sg["d_ossq"], 1)
                fill(23)

            pe.wait_ge(sg["d_free"], HEADS + 1)
            with pe.Fori(0, 8) as g:
                channel_group(pe, T_MRG + g, 0, U_MRG + g, ya, (0, 1))
                channel_group(pe, T_MRG + g, 1, U_MRG + g, yb, (2, 3))

            pe.wait_ge(sg["g_merged"], 9)
            with pe.Fori(0, 2) as it:
                for p in range(2):
                    for s in range(8):
                        token_slab(pe, T_OUT + it * 4 + p * 2 + s // 4, s % 4, p, U_OUT + it, hs, 2 * s, s == 0, s == 7)

            norm_pe(pe, 1, scaled)
            pe.wait_ge(lo_made, 2 * KD)
            with pe.Fori(0, 22) as g:
                channel_group(pe, T_FFN + g * 2, 0, U_FFN + g, hs)
                channel_group(pe, T_FFN + g * 2 + 1, 1, U_FFN + g, hs)

            pe.wait_ge(sg["hidden_ready"], 22)
            with pe.Fori(0, 2) as it:
                for n in range(44):
                    j = n % 22
                    token_slab(pe, T_DWN + it * 11 + n // 4, n % 4, n // 22, U_DWN + it, act_s, 2 * j, j == 0, j == 21)


def _slabs(w, rows, cols):
    k, n = w.shape
    v = w.reshape(k // (P * rows), rows, P, n // cols, cols)
    return v.transpose(3, 0, 2, 1, 4).reshape(n // cols, k // (P * rows), P, rows * cols)


def _constants(np):
    c = np.zeros((P, C_ALL), np.float32)
    i, j = np.arange(P)[:, None], np.arange(P)[None, :]
    chunk = i // CHUNK == j // CHUNK
    c[:, C_ID:C_ID + P] = i == j
    c[:, C_UP:C_UP + P] = chunk & (i <= j)
    c[:, C_SAME:C_SAME + P] = chunk
    for o in range(2):
        c[:, C_HALF + o * P:C_HALF + (o + 1) * P] = i // CHUNK == o
    for n in range(LEVELS):
        b = 1 << n
        c[:, C_LEVEL + n * P:C_LEVEL + (n + 1) * P] = (i // (2 * b) == j // (2 * b)) & (i % (2 * b) < b) & (j % (2 * b) >= b)
    causal = np.where(j <= i, 0.0, -1e30)
    c[:, C_CAUSAL:C_CAUSAL + P] = causal
    c[:, C_CAUSAL + 2 * P:C_CAUSAL + 3 * P] = causal
    return c


def kernel(**inputs):
    import numpy as np
    import concourse.bacc as bacc
    from concourse.bass_utils import run_bass_kernel_spmd

    a = {k: np.asarray(v) for k, v in inputs.items()}
    w_in, w_ffn = a["w_in"][0], a["w_ffn_in"][0]
    heads = HEADS * HD
    z0, b0, g0 = 6 * heads, 7 * heads, 7 * heads + 2 * HEADS
    flat = (-1, P, SLAB)

    def columns(v, n):
        return np.moveaxis(v.reshape(-1, n, P), 2, 0).transpose(0, 2, 1)

    in_slabs = [_slabs(w_in[:, c:c + n], 4, 256) for c, n in
                ((0, 3 * heads), (z0, heads), (3 * heads, 3 * heads), (g0, 2 * D))]
    dn = in_slabs[2].reshape(3, 4, 4, P, SLAB).transpose(1, 0, 2, 3, 4)
    branch = np.stack([_slabs(a["w_branch_a"][0], 4, 256), _slabs(a["w_branch_b"][0], 4, 256)], axis=1)
    gate, up = _slabs(w_ffn[:, :FF], 4, 256), _slabs(w_ffn[:, FF:], 4, 256)
    stream = np.concatenate([in_slabs[0].reshape(flat), in_slabs[1].reshape(flat), dn.reshape(flat),
                             in_slabs[3].reshape(flat), branch.reshape(flat),
                             _slabs(a["w_out"][0], 2, 512).reshape(flat),
                             np.stack([gate, up], axis=1).reshape(flat),
                             _slabs(a["w_ffn_down"][0], 2, 512).reshape(flat)])
    small = np.concatenate([
        a["attn_norm"][0].reshape(KD, P).T, a["ffn_norm"][0].reshape(KD, P).T,
        a["moba_q_norm"].reshape(P, 1), a["moba_k_norm"].reshape(P, 1), a["dn_out_norm"].reshape(P, 1),
        np.repeat(a["dn_a_log"].reshape(1, HEADS), P, axis=0), np.repeat(a["dn_dt_bias"].reshape(1, HEADS), P, axis=0),
        columns(a["dn_conv"][0], 3 * HEADS).reshape(P, -1), columns(a["ffn_conv"][0], KF).reshape(P, -1),
        a["ffn_conv_bias"][0].reshape(KF, P).T], axis=1)
    arrays = {
        "x": np.ascontiguousarray(a["x"][0]),
        "stream": np.ascontiguousarray(stream),
        "w_ba": np.ascontiguousarray(w_in[:, b0:g0].reshape(KD, P, 2 * HEADS).transpose(1, 0, 2)),
        "consts": _constants(np),
        "small": np.ascontiguousarray(small),
    }
    nc = bacc.Bacc("TRN2", target_bir_lowering=False, num_devices=1)
    args = [nc.dram_tensor(f"in_{n}", v.shape, F32, kind="ExternalInput").ap() for n, v in arrays.items()]
    out = nc.dram_tensor("out", (SEQ, D), F32, kind="ExternalOutput").ap()
    layer(nc, *args, out)
    r = run_bass_kernel_spmd(nc, [{f"in_{n}": v for n, v in arrays.items()}], core_ids=[0])
    return r.results[0]["out"].reshape(1, SEQ, D)
```

```python
from contextlib import ExitStack

import concourse.bass as bass
from concourse import mybir

P = 128
SEQ = 256
TOK = SEQ // P
D = 2048
KD = D // P
HEADS = 8
HD = 128
CHUNK = 64
NCH = SEQ // CHUNK
TAPS = 4
FF = 5632
KF = FF // P
FTAPS = 3
EPS = 1e-6
SCALE = HD ** -0.5

SLOTS = 4
SLAB = 1024
FILL = (0, 2, 3, 4, 1, 1, 1, 1, 1, 1, 1, 1, 1, 1, 1, 5, 1, 1, 1, 1, 1, 1, 1, 0)
MOBA_AT = (3, 10, 17, 21, 26, 32, 39, 44)
LEVELS = 6
AHEAD_HI, AHEAD_LO = 3, 2

T_IN1 = 0
T_IN2 = T_IN1 + 16
T_IN3 = T_IN2 + 12
T_MRG = T_IN3 + 16
T_OUT = T_MRG + 8
T_FFN = T_OUT + 8
T_DWN = T_FFN + 44
TURNS = T_DWN + 22
U_IN1, U_IN2, U_IN3, U_MRG, U_OUT, U_FFN, U_DWN = 0, 8, 12, 20, 28, 30, 52

C_ID, C_UP, C_SAME, C_HALF, C_LEVEL, C_CAUSAL = 0, 128, 256, 384, 640, 1408
C_ALL = 1792
S_ATTN = 0
S_FFN = S_ATTN + KD
S_QG = S_FFN + KD
S_KG = S_QG + 1
S_OG = S_KG + 1
S_ALOG = S_OG + 1
S_DT = S_ALOG + HEADS
S_CONV = S_DT + HEADS
S_FCONV = S_CONV + 3 * HEADS * TAPS
S_FBIAS = S_FCONV + KF * FTAPS
S_ALL = S_FBIAS + KF

F32 = mybir.dt.float32
F32R = mybir.dt.float32r
ACT = mybir.ActivationFunctionType
ALU = mybir.AluOpType
AX_X = mybir.AxisListType.X


def layer(nc, x, stream, w_ba, consts, small, out):
    with ExitStack() as ctx:
        def sb(name, shape, dt=F32):
            return ctx.enter_context(nc.sbuf_tensor(name, shape, dt))

        def sem(name):
            return ctx.enter_context(nc.semaphore(name))

        con = sb("constants", [P, C_ALL])
        par = sb("parameters", [P, S_ALL])
        raw = sb("w_raw", [P, SLOTS, SLAB])
        whi = sb("w_hi", [P, SLOTS, SLAB], F32R)
        wlo = sb("w_lo", [P, SLOTS, SLAB], F32R)
        hs = sb("act_split", [P, KD, 2, SEQ], F32R)
        half = sb("second_half", [P, 3, 2, SEQ])
        rstat = sb("row_stat", [P, 8, TOK])
        ident = con[:, C_ID:C_ID + P]

        def at_once(groups):
            made = []
            for group in groups:
                with ExitStack() as inner:
                    made.append([inner.enter_context(nc.sbuf_tensor(n, s, d)) for n, s, d in group])
            return made

        mixer = ExitStack()
        z = mixer.enter_context(nc.sbuf_tensor("z", [P, HEADS, SEQ], F32))
        ya = mixer.enter_context(nc.sbuf_tensor("y_moba", [P, HEADS, 2, SEQ], F32R))
        (dn,), (yb,) = at_once([[("dn_qkv", [P, HEADS + 1, 3, SEQ], F32)], [("y_dn", [P, HEADS, 3, SEQ], F32R)]])
        mixer.enter_context(nc.sbuf_tensor("dn_place", [P, HEADS + 1, 3, SEQ], F32))
        (xt,), (qkv,), (gates,) = at_once([[("x_tokens", [P, TOK, D], F32)],
                                           [("moba_qkv", [P, 3 * HEADS, SEQ], F32)],
                                           [("gates", [P, 2 * KD, SEQ], F32)]])
        mixer.enter_context(nc.sbuf_tensor("gates_place", [P, 2 * KD, SEQ], F32))
        gcol = mixer.enter_context(nc.sbuf_tensor("gate_columns", [P, TOK, 6, HEADS], F32))
        glast = mixer.enter_context(nc.sbuf_tensor("chunk_decay", [P, NCH, HEADS], F32))
        ones = mixer.enter_context(nc.sbuf_tensor("ones", [P, P], F32))
        moba_set = [("m_sq", [P, 2, SEQ], F32), ("m_rs", [P, 2, SEQ], F32), ("m_qn", [P, SEQ], F32),
                    ("m_kn", [P, SEQ], F32), ("m_v", [P, SEQ], F32), ("m_s", [P, 3 * P], F32),
                    ("m_mx", [P, 8], F32), ("m_pt", [P, 3 * P], F32), ("m_vt", [P, TOK, P], F32),
                    ("conv_in", [P, 2, TAPS - 1 + SEQ], F32), ("conv_acc", [P, 2, SEQ], F32)]
        dn_set = [("d_sq", [P, 2, SEQ], F32), ("d_qn", [P, SEQ], F32), ("d_kn", [P, SEQ], F32),
                  ("d_v", [P, SEQ], F32), ("d_cast", [P, 2, TOK, P], F32), ("d_kb", [P, SEQ], F32),
                  ("d_e", [P, TOK, P], F32), ("d_qg", [P, SEQ], F32), ("d_lv", [P, LEVELS, TOK, P], F32),
                  ("d_tu", [P, 2, TOK, P], F32), ("d_p", [P, TOK, P], F32), ("d_vb", [P, TOK, P], F32),
                  ("d_kbg", [P, TOK, P], F32), ("d_kd", [P, TOK, P], F32), ("d_uw", [P, 2, TOK, P], F32),
                  ("d_at", [P, TOK, P], F32), ("d_vn", [P, TOK, P], F32),
                  ("d_state", [P, P], F32)]
        start_set = [("wba", [P, KD, 2 * HEADS], F32), ("wba_hi", [P, KD, 2 * HEADS], F32R),
                     ("wba_lo", [P, KD, 2 * HEADS], F32R), ("gt", [P, 6, TOK, HEADS], F32), ("ba", [P, 2, SEQ], F32)]
        m_all, d_all, s_all = at_once([moba_set, dn_set, start_set])
        m_sq, m_rs, m_qn, m_kn, m_v, m_s, m_mx, m_pt, m_vt, cin, cacc = m_all
        (d_sq, d_qn, d_kn, d_v, d_cast, d_kb, d_e, d_qg, d_lv, d_tu, d_p, d_vb, d_kbg, d_kd, d_uw, d_at, d_vn,
         d_state) = d_all
        d_on = d_uw[:, :, :, :].rearrange("p a t d -> p a (t d)")
        wba, wbah, wbal, gt, ba = s_all
        mixer.close()
        x1 = sb("residual", [P, TOK, D])
        (scaled,), (act_s,) = at_once([[("x1_scaled", [P, TOK, D], F32)], [("hidden_split", [P, KF, 2, SEQ], F32R)]])
        sb("hidden_place", [P, KF, 2, SEQ])
        fin = sb("ffn_conv_in", [P, 2, FTAPS - 1 + SEQ])
        facc = sb("ffn_acc", [P, 2, SEQ])
        mg = z[:, :, :].rearrange("p (a c) t -> p a (c t)", c=2)

        ps = ctx.enter_context(nc.psum_tensor("ps", [P, 8, 512], F32))

        def pair(p):
            return ps[:, 2 * p:2 * p + 2, :].rearrange("p c (h t) -> p c h t", h=2)

        raw_loaded = [sem(f"raw_loaded{s}") for s in range(SLOTS)]
        hi_ready, lo_ready = sem("hi_ready"), sem("lo_ready")
        slabs_used = sem("slabs_used")
        pair_free = [sem(f"pair_free{p}") for p in range(3)]
        half_copied = [sem(f"half_copied{p}") for p in range(3)]
        x_loaded = [sem(f"x_loaded{t}") for t in range(TOK)]
        first_loaded, tables_loaded, x1_loaded = sem("first_loaded"), sem("tables_loaded"), sem("x1_loaded")
        ones_set = sem("ones_set")
        row_sq, row_log, row_rstd = sem("row_sq"), sem("row_log"), sem("row_rstd")
        row_scaled = [sem(f"row_scaled{t}") for t in range(TOK)]
        turned, hi_made, lo_made = sem("turned"), sem("hi_made"), sem("lo_made")
        ba_hi, ba_lo, ba_done = sem("ba_hi"), sem("ba_lo"), sem("ba_done")
        ba_half, ba_added, ba_turned = sem("ba_half"), sem("ba_added"), sem("ba_turned")
        gate_v, gate_a, gate_sums, gates_ready = sem("gate_v"), sem("gate_a"), sem("gate_sums"), sem("gates_ready")
        names = ("m_free m_squares m_ssq m_log m_rstd m_qn_ready m_v_ready m_scores m_vturned m_masked m_max m_bias "
                 "m_exp m_rinv m_prob m_pturned m_pt_ready m_vt_ready m_out m_hi "
                 "c_zero c_tap c_acc c_sum silu_done "
                 "d_pad d_free d_squares d_ssq d_log d_rstd d_cast_ready d_v_ready d_norm d_rows d_tok d_kb_ready d_prod "
                 "d_arg d_exp d_egrow d_lv0_ready d_qg_ready d_incl d_amat d_attn d_levels d_vb_ready d_kbg_ready d_kd_ready "
                 "d_l0 d_t_ready d_u_level d_p_done d_p_ready d_tp_done d_pu_done d_uw d_u_ready "
                 "d_ws d_vn_ready d_okv d_state_ready d_osq d_ossq d_olog d_orstd d_on d_y d_yhi "
                 "g_sig g_mul g_merged g_hi merged "
                 "f_zero f_tap f_acc f_silu f_prod f_hi hidden_ready "
                 "x1_added x1_sq stat_sum y_added y_stored last_stored").split()
        sg = {n: sem(n) for n in names}

        block = ctx.enter_context(nc.Block())

        def ahead(turn, s, by):
            return turn + (s + by) // SLOTS, (s + by) % SLOTS

        def cast(act, turn, s):
            cast_slab(act, *ahead(turn, s, AHEAD_HI))

        def cast_slab(act, turn, s):
            act.wait_ge(raw_loaded[s], (turn + 1) * 16)
            act.wait_ge(slabs_used, turn * SLOTS + s + 1)
            act.activation(whi[:, s], raw[:, s], ACT.Copy).then_inc(hi_ready, 1)

        def split(dve, turn, s):
            split_slab(dve, *ahead(turn, s, AHEAD_LO))

        def split_slab(dve, turn, s):
            dve.wait_ge(hi_ready, turn * SLOTS + s + 1)
            dve.tensor_tensor(wlo[:, s], raw[:, s], whi[:, s].bitcast(F32), ALU.subtract).then_inc(lo_ready, 1)

        def channel_unit(pe, turn, s, k, p, use, xs, kx, first, last):
            if k == 0:
                pe.wait_ge(lo_ready, turn * SLOTS + s + 1)
            if first:
                pe.wait_ge(pair_free[p], use + 1)
            both = xs[:, kx, 0:2, :].rearrange("p a t -> p (a t)")
            for c in range(2):
                at = k * 256 + c * P
                bank = ps[:, 2 * p + c, :]

                def lo_product():
                    return pe.matmul(bank[:, 0:SEQ], wlo[:, s, at:at + P], xs[:, kx, 0, :], start=False, stop=False,
                                     skip_group_check=True)
                if first:
                    pe.matmul(bank, whi[:, s, at:at + P], both, start=True, stop=False)
                    mm = lo_product()
                else:
                    lo_product()
                    mm = pe.matmul(bank, whi[:, s, at:at + P], both, start=False, stop=last)
            if k == 3:
                mm.then_inc(slabs_used, 1)

        def channel_group(pe, turn, p, use, xs, slots=(0, 1, 2, 3)):
            n = 4 * len(slots)
            for j in range(n):
                channel_unit(pe, turn, slots[j // 4], j % 4, p, use, xs, j, j == 0, j == n - 1)

        def multiplied(eng, turn, s=SLOTS - 1):
            eng.wait_ge(slabs_used, SLOTS + turn * SLOTS + s + 1)

        def read_out(eng, p, use):
            eng.wait_ge(pair_free[p], use + 2)

        def copy_half(act, p, turn, s=SLOTS - 1):
            multiplied(act, turn, s)
            act.activation(half[:, p], pair(p)[:, :, 1, :], ACT.Copy).then_inc(half_copied[p], 1)

        def add_halves(dve, p, use, dest, without=0):
            dve.wait_ge(half_copied[p], use - without + 1)
            return dve.tensor_tensor(dest, pair(p)[:, :, 0, :], half[:, p], ALU.add).then_inc(pair_free[p], 1)

        def token_slab(pe, turn, s, p, use, xs, kx, first, last):
            pe.wait_ge(lo_ready, turn * SLOTS + s + 1)
            if first:
                pe.wait_ge(pair_free[p], use + 1)
            for k in range(2):
                w_h, w_l = whi[:, s, k * 512:(k + 1) * 512], wlo[:, s, k * 512:(k + 1) * 512]
                for t in range(TOK):
                    bank = ps[:, 2 * p + t, :]
                    x_h, x_l = xs[:, kx + k, 0, t * P:(t + 1) * P], xs[:, kx + k, 1, t * P:(t + 1) * P]
                    pe.matmul(bank, x_h, w_l, start=first and k == 0, stop=False)
                    pe.matmul(bank, x_h, w_h, start=False, stop=False)
                    mm = pe.matmul(bank, x_l, w_h, start=False, stop=last and k == 1)
            mm.then_inc(slabs_used, 1)

        def per_tile(mask):
            return mask.unsqueeze(1).to_broadcast([P, TOK, P])

        TURN_BANKS = 6

        def turned_block(k):
            return ps[:, 2 + k % TURN_BANKS, 0:SEQ]

        def norm_act(act, n, gain, src, dest, turn, slabs):
            act.activation(rstat[:, 5, :], rstat[:, 4, :], ACT.Ln, scale=1.0 / D, bias=rstat[:, 7, 0:1])\
               .then_inc(row_log, 1)
            act.wait_ge(row_log, n + 1)
            act.activation(rstat[:, 6, :], rstat[:, 5, :], ACT.Exp, scale=-0.5).then_inc(row_rstd, 1)
            act.wait_ge(row_rstd, n + 1)
            for c in range(0, D, D // 4):
                act.activation(dest[:, 1, c:c + D // 4], src[:, 1, c:c + D // 4], ACT.Copy, scale=rstat[:, 6, 1:2])\
                   .then_inc(row_scaled[1], 1)
            if n == 0:
                act.wait_ge(first_loaded, 32)
            for k in range(KD):
                if k in slabs:
                    cast_slab(act, turn, slabs[k])
                act.wait_ge(turned, n * KD + k + 1)
                act.activation(hs[:, k, 0, :], turned_block(k), ACT.Copy,
                               scale=par[:, gain + k:gain + k + 1]).then_inc(hi_made, 1)

        def norm_dve(dve, n, gain, src, dest, turn, slabs):
            dve.wait_ge(row_rstd, n + 1)
            for c in range(0, D, D // 4):
                dve.tensor_scalar(dest[:, 0, c:c + D // 4], src[:, 0, c:c + D // 4], rstat[:, 6, 0:1], None, ALU.mult)\
                   .then_inc(row_scaled[0], 1)
            for k in range(KD):
                dve.wait_ge(hi_made, n * KD + k + 1)
                dve.scalar_tensor_tensor(out=hs[:, k, 1, :],
                                         in0=turned_block(k),
                                         scalar=par[:, gain + k:gain + k + 1], in1=hs[:, k, 0, :].bitcast(F32),
                                         op0=ALU.mult, op1=ALU.subtract).then_inc(lo_made, 1)
                if k in slabs:
                    split_slab(dve, turn, slabs[k])

        def norm_pe(pe, n, scaled, turn, use):
            for k in range(KD + TURN_BANKS):
                if k < KD and k % 4 == 0:
                    for t in range(TOK):
                        pe.wait_ge(row_scaled[t], 4 * n + k // 4 + 1)
                done = k - TURN_BANKS
                if done >= 0:
                    pe.wait_ge(lo_made, n * KD + done + 1)
                if k < KD:
                    for t in range(TOK):
                        mm = pe.transpose(turned_block(k)[:, t * P:(t + 1) * P], scaled[:, t, k * P:(k + 1) * P], ident)
                    mm.then_inc(turned, 1)
                if done >= 0:
                    channel_unit(pe, turn, done // 4, done % 4, 0, use, hs, done, done == 0, done == KD - 1)

        @block.sync
        def _(sp):
            for t in range(TOK):
                sp.dma_start(xt[:, t, :], x[t * P:(t + 1) * P, :]).then_inc(x_loaded[t], 16)
            sp.dma_start(ident, consts[:, C_ID:C_ID + P]).then_inc(first_loaded, 16)
            sp.dma_start(par[:, :], small).then_inc(first_loaded, 16)
            for s in range(SLOTS):
                sp.dma_start(raw[:, s], stream[s]).then_inc(raw_loaded[s], 16)
            sp.dma_start(wba[:, :, :], w_ba).then_inc(tables_loaded, 16)
            sp.dma_start(con[:, C_UP:], consts[:, C_UP:]).then_inc(tables_loaded, 16)
            with sp.Fori(1, TURNS) as turn:
                for s in range(SLOTS):
                    sp.wait_ge(lo_ready, turn * SLOTS + (s - SLOTS + 1))
                    sp.dma_start(raw[:, s], stream[bass.ds(turn * SLOTS + s, 1)].rearrange("o p n -> p (o n)"))\
                      .then_inc(raw_loaded[s], 16)
            sp.wait_ge(sg["y_stored"], 16 * 3 * TOK)
            sp.wait_ge(sg["last_stored"], 16 * TOK)

        @block.gpsimd
        def _(pool):
            pool.memset(ones[:, :], 1.0).then_inc(ones_set, 1)
            pool.wait_ge(gates_ready, 2)
            pool.memset(cin[:, :, 0:TAPS - 1], 0.0).then_inc(sg["c_zero"], 1)
            pool.memset(dn[:, HEADS, :, :], 0.0).then_inc(sg["d_pad"], 1)
            pool.wait_ge(sg["m_free"], HEADS + 1)
            pool.wait_ge(sg["c_sum"], 12)
            with pool.Fori(0, HEADS) as h:
                for j in range(2):
                    for t in range(TOK):
                        ins = pool.tensor_copy(d_cast[:, j, t, :], gcol[:, t, j, bass.ds(h, 1)].to_broadcast([P, P]))
                ins.then_inc(sg["d_cast_ready"], 1)
                pool.wait_ge(sg["d_exp"], h + 1)
                pool.tensor_tensor(d_p[:, :, :], d_e[:, :, :], per_tile(con[:, C_UP:C_UP + P]), ALU.mult)\
                    .then_inc(sg["d_incl"], 1)
                pool.wait_ge(sg["d_amat"], h + 1)
                for j in range(1, LEVELS):
                    pool.tensor_tensor(d_lv[:, j], d_vn[:, :, :], per_tile(con[:, C_LEVEL + j * P:C_LEVEL + (j + 1) * P]),
                                       ALU.mult).then_inc(sg["d_levels"], 1)
                pool.wait_ge(sg["d_egrow"], h + 1)
                pool.tensor_tensor(d_qg[:, :], d_qg[:, :], d_qn[:, :], ALU.mult).then_inc(sg["d_qg_ready"], 1)
            pool.wait_ge(sg["g_merged"], 9)
            pool.dma_start(x1[:, :, :], x.rearrange("(t p) d -> p t d", p=P)).then_inc(x1_loaded, 16)
            for cb in range(3):
                for t in range(TOK):
                    if t == 0:
                        pool.wait_ge(sg["y_added"], cb + 1)
                    else:
                        read_out(pool, cb % 2, U_DWN + cb // 2)
                    pool.dma_start(out[t * P:(t + 1) * P, cb * 512:(cb + 1) * 512], x1[:, t, cb * 512:(cb + 1) * 512])\
                        .then_inc(sg["y_stored"], 16)

        @block.scalar
        def _(act):
            nc.scalar.preload_act_table_set("natural_log_exp_and_others")
            for t in range(TOK):
                act.wait_ge(x_loaded[t], 16)
                act.activation(hs[:, 4 * t:4 * t + 4, :, :].rearrange("p a b c -> p (a b c)"), xt[:, t, :], ACT.Square,
                               accum_out=rstat[:, 4, t:t + 1]).then_inc(row_sq, 1)
            act.wait_ge(row_sq, TOK + 1)
            norm_act(act, 0, S_ATTN, xt, xt, T_IN1, {0: 0, 3: 1, 7: 2, 11: 3})
            act.wait_ge(tables_loaded, 32)
            act.activation(wbah[:, :, :], wba[:, :, :], ACT.Copy).then_inc(ba_hi, 1)

            def gate_half(act):
                act.wait_ge(ba_done, 1)
                act.activation(ba[0:2 * HEADS, 1, :], ps[0:2 * HEADS, 6, SEQ:2 * SEQ], ACT.Copy).then_inc(ba_half, 1)

            def gate_exps(act):
                act.wait_ge(ba_turned, 1)
                act.activation(gt[:, 1], ps[:, 6, 0:TOK * 2 * HEADS].rearrange("p (t j) -> p t j", t=TOK)[:, :, 0:HEADS],
                               ACT.Exp, scale=-1.0).then_inc(gate_a, 1)
                act.activation(gt[:, 4, 0, :], par[:, S_ALOG:S_ALOG + HEADS], ACT.Exp).then_inc(gate_a, 1)

            def gate_abs(act):
                act.wait_ge(gate_v, 2)
                act.activation(gt[:, 3], gt[:, 2], ACT.Exp, scale=-1.0).then_inc(gate_a, 1)

            def gate_log(act):
                act.wait_ge(gate_a, 3)
                act.activation(gt[:, 2], gt[:, 3], ACT.Ln, bias=1.0).then_inc(gate_a, 1)

            def gate_decays(act):
                act.wait_ge(gate_sums, 1)
                act.activation(glast[:, :, :], ps[:, 7, 64:64 + NCH * HEADS].rearrange("p (c h) -> p c h", c=NCH),
                               ACT.Exp)
                act.activation(gcol[:, :, 2, :], ps[:, 7, 0:TOK * HEADS].rearrange("p (t h) -> p t h", t=TOK), ACT.Copy)\
                   .then_inc(gate_a, 1)
                act.activation(gt[:, 5], ps[:, 7, 0:TOK * HEADS].rearrange("p (t h) -> p t h", t=TOK), ACT.Exp)\
                   .then_inc(gate_a, 1)

            def in1_pair(act, it, between, made=0):
                for p in range(2):
                    for s in range(SLOTS):
                        if p * SLOTS + s >= made:
                            cast(act, T_IN1 + it * 2 + p, s)
                        if s == 0 and p == 1:
                            copy_half(act, 0, T_IN1 + it * 2)
                        if (p, s) in between:
                            between[p, s](act)
                copy_half(act, 1, T_IN1 + it * 2 + 1)

            in1_pair(act, 0, {}, SLOTS - AHEAD_HI)
            with act.Fori(1, 6) as it:
                in1_pair(act, it, {})
            in1_pair(act, 6, {(0, 2): gate_half, (1, 2): gate_exps})
            in1_pair(act, 7, {(0, 0): gate_abs, (0, 1): gate_log, (1, 2): gate_decays})
            act.wait_ge(gate_v, 5)
            act.activation(gcol[:, :, 4, :], gt[:, 0], ACT.Exp).then_inc(gates_ready, 1)

            def moba_squares(act, h):
                act.activation(m_sq[:, 0, :], qkv[:, bass.ds(h, 1), :].rearrange("p o t -> p (o t)"), ACT.Square)
                act.activation(m_sq[:, 1, :], qkv[:, bass.ds(h + HEADS, 1), :].rearrange("p o t -> p (o t)"),
                               ACT.Square).then_inc(sg["m_squares"], 1)

            def moba_reply(act, j, h):
                if j == 0:
                    act.activation(m_v[:, :], qkv[:, bass.ds(h + 2 * HEADS, 1), :].rearrange("p o t -> p (o t)"),
                                   ACT.Copy).then_inc(sg["m_v_ready"], 1)
                    act.wait_ge(sg["m_ssq"], h + 1)
                    act.activation(m_rs[:, :, :], ps[:, 6, :].rearrange("p (a t) -> p a t", a=2), ACT.Ln,
                                   scale=1.0 / HD, bias=rstat[:, 7, 0:1]).then_inc(sg["m_log"], 1)
                    act.wait_ge(sg["m_log"], h + 1)
                    act.activation(m_rs[:, :, :], m_rs[:, :, :], ACT.Exp, scale=-0.5).then_inc(sg["m_rstd"], 1)
                if j == 1:
                    act.wait_ge(sg["m_vturned"], h + 1)
                    act.activation(m_vt[:, :, :], ps[:, 6, 0:SEQ].rearrange("p (t d) -> p t d", t=TOK), ACT.Copy)\
                       .then_inc(sg["m_vt_ready"], 1)
                    act.wait_ge(sg["m_bias"], h + 1)
                    act.activation(m_s[:, 0:P], m_s[:, 0:P], ACT.Exp, scale=SCALE, bias=m_mx[:, 2:3],
                                   accum_out=m_mx[:, 4:5])
                    act.activation(m_s[:, P:3 * P], m_s[:, P:3 * P], ACT.Exp, scale=SCALE, bias=m_mx[:, 3:4],
                                   accum_out=m_mx[:, 5:6]).then_inc(sg["m_exp"], 1)
                if j == 2:
                    act.wait_ge(sg["m_pturned"], h + 1)
                    act.activation(m_pt[:, :], ps[:, 7, 0:3 * P], ACT.Copy).then_inc(sg["m_pt_ready"], 1)
                if j == 3:
                    act.wait_ge(sg["m_out"], h + 1)
                    act.activation(ya[:, bass.ds(h, 1), 0, :].rearrange("p o t -> p (o t)"), ps[:, 6, SEQ:2 * SEQ],
                                   ACT.Copy).then_inc(sg["m_hi"], 1)

            def conv_first_tap(act, it, g):
                read_out(act, g, it + (U_IN2 if g < 2 else 0))
                for c in range(2):
                    w = S_CONV + g * HEADS * TAPS
                    act.activation(cacc[:, c, :], cin[:, c, 0:SEQ], ACT.Copy,
                                   scale=par[:, bass.ds(w + (it * 2 + c) * TAPS, 1)]).then_inc(sg["c_tap"], 1)

            read_out(act, 1, U_IN2 - 1)
            moba_squares(act, 0)
            with act.Fori(0, 4) as it:
                for m in range(12):
                    if m == 10:
                        act.wait_ge(sg["c_sum"], it * 3 + 2)
                    cast(act, T_IN2 + it * 3 + m // 4, m % 4)
                    for j in range(8):
                        if MOBA_AT[j] // 4 == m:
                            moba_reply(act, j % 4, it * 2 + j // 4)
                            if j % 4 == 2:
                                moba_squares(act, it * 2 + j // 4 + 1)
                    if m in (4, 8):
                        g = m // 4 - 1
                        copy_half(act, g, T_IN2 + it * 3 + g)
                        conv_first_tap(act, it, g)
                    if m == 10:
                        nc.scalar.preload_act_table_set("silu_and_others")
                        part = dn[:, bass.ds(it * 2, 2), 0:2, :]
                        act.activation(part, part, ACT.Silu)
                        part = z[:, bass.ds(it * 2, 2), :]
                        act.activation(part, part, ACT.Silu)
                        nc.scalar.preload_act_table_set("natural_log_exp_and_others")
                copy_half(act, 2, T_IN2 + it * 3 + 2)
                conv_first_tap(act, it, 2)

            act.wait_ge(sg["m_free"], HEADS + 1)
            act.wait_ge(sg["m_squares"], HEADS + 1)
            act.wait_ge(sg["d_pad"], 1)

            def head_squares(act, h):
                act.activation(d_sq[:, :, :], dn[:, bass.ds(h, 1), 0:2, :].rearrange("p o a t -> p (o a) t"), ACT.Square)\
                   .then_inc(sg["d_squares"], 1)

            def head_rstd(act, h):
                act.wait_ge(sg["d_ssq"], h + 1)
                act.activation(d_sq[:, :, :], ps[:, 7, :].rearrange("p (a t) -> p a t", a=2), ACT.Ln,
                               bias=rstat[:, 7, 0:1]).then_inc(sg["d_log"], 1)
                act.wait_ge(sg["d_log"], h + 1)
                act.activation(d_sq[:, :, :], d_sq[:, :, :], ACT.Exp, scale=-0.5).then_inc(sg["d_rstd"], 1)

            def head_v(act, h):
                act.activation(d_v[:, :], dn[:, bass.ds(h, 1), 2, :].rearrange("p o t -> p (o t)"), ACT.Copy)\
                   .then_inc(sg["d_v_ready"], 1)

            head_squares(act, 0)
            head_rstd(act, 0)
            nc.scalar.preload_act_table_set("silu_and_others")
            for h, convs in ((0, 9), (HEADS - 2, 12)):
                act.wait_ge(sg["c_sum"], convs)
                part = dn[:, h:h + 2 if h else HEADS - 2, 2, :]
                act.activation(part, part, ACT.Silu).then_inc(sg["silu_done"], 1)
            nc.scalar.preload_act_table_set("natural_log_exp_and_others")
            act.wait_ge(sg["silu_done"], 2)
            head_v(act, 0)
            with act.Fori(0, HEADS) as h:
                def step(m):
                    cast(act, T_IN3 + h * 2 + m // 4, m % 4)

                step(0)
                act.wait_ge(sg["d_arg"], h + 1)
                act.activation(d_e[:, :, :], d_e[:, :, :], ACT.Exp).then_inc(sg["d_exp"], 1)
                act.activation(d_qg[:, :], ps[:, 5, 0:SEQ], ACT.Exp).then_inc(sg["d_egrow"], 1)
                step(1)
                act.wait_ge(sg["d_tok"], h + 1)
                for t in range(TOK):
                    act.activation(d_vb[:, t, :], ps[:, 6, SEQ + t * P:SEQ + (t + 1) * P], ACT.Copy,
                                   scale=gcol[:, t, 1, bass.ds(h, 1)]).then_inc(sg["d_vb_ready"], 1)
                for t in range(TOK):
                    act.activation(d_kbg[:, t, :], ps[:, 6, t * P:(t + 1) * P], ACT.Copy,
                                   scale=gcol[:, t, 3, bass.ds(h, 1)]).then_inc(sg["d_kbg_ready"], 1)
                for j in range(1, LEVELS):
                    act.wait_ge(sg["d_p_done"], h * (LEVELS - 1) + j)
                    act.activation(d_p[:, :, :], ps[:, 4, 0:SEQ].rearrange("p (t d) -> p t d", t=TOK), ACT.Copy)\
                       .then_inc(sg["d_p_ready"], 1)
                    if j in (1, 2, 4, 5):
                        step({1: 2, 2: 3, 4: 4, 5: 5}[j])
                    if j == 4:
                        copy_half(act, 0, T_IN3 + h * 2)
                act.wait_ge(sg["d_free"], h + 1)
                act.wait_ge(sg["d_uw"], h + 1)
                act.activation(d_uw[:, :, :, :], ps[:, 7, :].rearrange("p (a t d) -> p a t d", a=2, t=TOK), ACT.Copy)\
                   .then_inc(sg["d_u_ready"], 1)
                head_squares(act, h + 1)
                step(6)
                head_v(act, h + 1)
                head_rstd(act, h + 1)
                step(7)
                act.wait_ge(sg["d_okv"], h * NCH + NCH)
                act.activation(d_on[:, 0, :], ps[:, 6, 0:SEQ], ACT.Square).then_inc(sg["d_osq"], 1)
                act.wait_ge(sg["d_ossq"], h + 1)
                act.activation(d_on[:, 1, :], ps[:, 7, 0:SEQ], ACT.Ln, scale=1.0 / HD, bias=rstat[:, 7, 0:1])\
                   .then_inc(sg["d_olog"], 1)
                act.wait_ge(sg["d_olog"], h + 1)
                act.activation(d_on[:, 1, :], d_on[:, 1, :], ACT.Exp, scale=-0.5).then_inc(sg["d_orstd"], 1)
                copy_half(act, 1, T_IN3 + h * 2 + 1)

            read_out(act, 1, U_MRG - 1)
            nc.scalar.preload_act_table_set("sigmoid_and_others")
            with act.Fori(0, 8) as g:
                sig = mg[:, 0:2, :].rearrange("p a (b t) -> p (a b) t", t=SEQ)

                def gate(j):
                    act.activation(sig[:, 2 * j:2 * j + 2], gates[:, bass.ds(g * 2 + j * KD, 2), :], ACT.Sigmoid)\
                       .then_inc(sg["g_sig"], 1)
                for s in range(SLOTS):
                    cast(act, T_MRG + g, s)
                    if s == 0:
                        gate(0)
                    if s == 1:
                        gate(1)
                    if s == 2:
                        copy_half(act, 0, T_MRG + g, 1)
                copy_half(act, 1, T_MRG + g)
                act.wait_ge(sg["merged"], g + 1)
                act.activation(hs[:, bass.ds(g * 2, 2), 0, :], mg[:, 2, :].rearrange("p (b t) -> p b t", t=SEQ), ACT.Copy)\
                   .then_inc(sg["g_hi"], 1)

            nc.scalar.preload_act_table_set("natural_log_exp_and_others")

            def new_squares(act, p, it):
                for t in range(TOK):
                    if t == 0:
                        act.wait_ge(sg["x1_added"], it * 2 + p + 1)
                    else:
                        read_out(act, p, U_OUT + it)
                    act.wait_ge(sg["x1_sq"], it * 4 + p * TOK + t + 1)
                    act.activation(half[:, 0].rearrange("p a t -> p (a t)"), x1[:, t, bass.ds(it * 1024 + p * 512, 512)],
                                   ACT.Square, accum_out=rstat[:, bass.ds(it * 2 + p, 1), t]).then_inc(sg["x1_sq"], 1)
            with act.Fori(0, 2) as it:
                for p in range(2):
                    for s in range(8):
                        cast(act, T_OUT + it * 4 + p * 2 + s // 4, s % 4)
                        if p == 1 and s == 2:
                            new_squares(act, 0, it)
                new_squares(act, 1, it)
            act.wait_ge(sg["stat_sum"], 1)
            norm_act(act, 1, S_FFN, x1, scaled, T_FFN, {8: 3})

            nc.scalar.preload_act_table_set("silu_and_others")
            def ffn_group(act, g, made=0):
                for m in range(8):
                    if m >= made:
                        cast(act, T_FFN + g * 2 + m // 4, m % 4)
                    if m == 4:
                        copy_half(act, 0, T_FFN + g * 2)
                        read_out(act, 0, U_FFN + g)
                        for c in range(2):
                            act.activation(facc[:, c, :], fin[:, c, 0:SEQ], ACT.Identity,
                                           scale=par[:, bass.ds(S_FCONV + (g * 2 + c) * FTAPS, 1)],
                                           bias=par[:, bass.ds(S_FBIAS + g * 2 + c, 1)]).then_inc(sg["f_tap"], 1)
                    if m == 5:
                        act.wait_ge(sg["f_acc"], (g + 1) * 4)
                        act.activation(facc[:, :, :], facc[:, :, :], ACT.Silu).then_inc(sg["f_silu"], 1)
                copy_half(act, 1, T_FFN + g * 2 + 1)
                act.wait_ge(sg["f_prod"], g + 1)
                act.activation(act_s[:, bass.ds(g * 2, 2), 0, :], facc[:, :, :], ACT.Copy).then_inc(sg["f_hi"], 1)

            ffn_group(act, 0, SLOTS - AHEAD_HI)
            with act.Fori(1, 22) as g:
                ffn_group(act, g)

            with act.Fori(0, 21) as turn:
                for s in range(SLOTS):
                    cast(act, T_DWN + turn, s)
            cast(act, T_DWN + 21, 0)
            for t in range(TOK):
                if t == 0:
                    act.wait_ge(sg["y_added"], 4)
                else:
                    read_out(act, 1, U_DWN + 1)
                act.dma_start(out[t * P:(t + 1) * P, 3 * 512:4 * 512], x1[:, t, 3 * 512:4 * 512])\
                   .then_inc(sg["last_stored"], 16)

        @block.vector
        def _(dve):
            dve.memset(rstat[:, 7, :], EPS).then_inc(row_sq, 1)
            dve.sem_inc(slabs_used, SLOTS)
            for p in range(3):
                dve.sem_inc(pair_free[p], 1)
            dve.sem_inc(sg["m_free"], 1)
            dve.sem_inc(sg["d_free"], 1)
            dve.sem_inc(sg["d_on"], 1)
            dve.sem_inc(sg["g_merged"], 1)
            dve.sem_inc(sg["x1_sq"], 1)
            norm_dve(dve, 0, S_ATTN, xt, xt, T_IN1, {0: 0, 3: 1, 7: 2, 11: 3})
            dve.wait_ge(ba_hi, 1)
            dve.tensor_tensor(wbal[:, :, :], wba[:, :, :], wbah[:, :, :].bitcast(F32), ALU.subtract).then_inc(ba_lo, 1)

            def gate_add(dve):
                dve.wait_ge(ba_half, 1)
                dve.tensor_tensor(ba[0:2 * HEADS, 0, :], ps[0:2 * HEADS, 6, 0:SEQ], ba[0:2 * HEADS, 1, :], ALU.add)\
                   .then_inc(ba_added, 1)

            def gate_input(dve):
                dve.wait_ge(gate_a, 1)
                a_in = ps[:, 6, 0:TOK * 2 * HEADS].rearrange("p (t j) -> p t j", t=TOK)[:, :, HEADS:2 * HEADS]
                for t in range(TOK):
                    ins = dve.tensor_tensor(gt[:, 0, t, :], a_in[:, t, :], par[:, S_DT:S_DT + HEADS], ALU.add)
                ins.then_inc(gate_v, 1)
                dve.wait_ge(gate_v, 1)
                dve.scalar_tensor_tensor(out=gt[:, 2], in0=gt[:, 0], scalar=-1.0, in1=gt[:, 0], op0=ALU.mult,
                                         op1=ALU.max).then_inc(gate_v, 1)

            def gate_values(dve):
                dve.wait_ge(gate_a, 4)
                dve.tensor_scalar(gt[:, 1], gt[:, 1], 1.0, None, ALU.add)
                dve.scalar_tensor_tensor(out=gt[:, 5], in0=gt[:, 0], scalar=0.0, in1=gt[:, 2], op0=ALU.max, op1=ALU.add)\
                   .then_inc(gate_v, 1)
                dve.wait_ge(gate_v, 3)
                dve.reciprocal(gcol[:, :, 1, :], gt[:, 1])
                for t in range(TOK):
                    ins = dve.scalar_tensor_tensor(out=gcol[:, t, 0, :], in0=gt[:, 5, t, :], scalar=-1.0,
                                                   in1=gt[:, 4, 0, :], op0=ALU.mult, op1=ALU.mult)
                ins.then_inc(gate_v, 1)

            def gate_products(dve):
                dve.wait_ge(gate_a, 6)
                dve.tensor_tensor(gt[:, 0], ps[:, 7, 32:32 + TOK * HEADS].rearrange("p (t h) -> p t h", t=TOK),
                                  gcol[:, :, 2, :], ALU.subtract).then_inc(gate_v, 1)
                dve.tensor_tensor(gcol[:, :, 3, :], gt[:, 5], gcol[:, :, 1, :], ALU.mult).then_inc(gates_ready, 1)

            def in1_pair(dve, it, dest, to, between, made=0):
                for p in range(2):
                    for s in range(SLOTS):
                        if p * SLOTS + s >= made:
                            split(dve, T_IN1 + it * 2 + p, s)
                        if s == 0 and p == 1:
                            add_halves(dve, 0, U_IN1 + it, dest[:, bass.ds(to * 4, 2), :])
                        if (p, s) in between:
                            between[p, s](dve)
                add_halves(dve, 1, U_IN1 + it, dest[:, bass.ds(to * 4 + 2, 2), :])
            in1_pair(dve, 0, qkv, 0, {}, SLOTS - AHEAD_LO)
            with dve.Fori(1, 6) as it:
                in1_pair(dve, it, qkv, it, {})
            in1_pair(dve, 6, z, 0, {(0, 2): gate_add, (1, 2): gate_input})
            in1_pair(dve, 7, z, 1, {(0, 1): gate_values, (1, 2): gate_products})

            def moba_reply(dve, j, h):
                if j == 0:
                    dve.wait_ge(sg["m_rstd"], h + 1)
                    dve.scalar_tensor_tensor(out=m_qn[:, :], in0=qkv[:, bass.ds(h, 1), :].rearrange("p o t -> p (o t)"),
                                             scalar=par[:, S_QG:S_QG + 1], in1=m_rs[:, 0, :], op0=ALU.mult,
                                             op1=ALU.mult)
                    dve.scalar_tensor_tensor(out=m_kn[:, :],
                                             in0=qkv[:, bass.ds(h + HEADS, 1), :].rearrange("p o t -> p (o t)"),
                                             scalar=par[:, S_KG:S_KG + 1], in1=m_rs[:, 1, :], op0=ALU.mult,
                                             op1=ALU.mult).then_inc(sg["m_qn_ready"], 1)
                if j == 1:
                    dve.wait_ge(sg["m_scores"], h + 1)
                    dve.tensor_tensor(m_s[:, :], ps[:, 7, 0:3 * P], con[:, C_CAUSAL:C_CAUSAL + 3 * P], ALU.add)\
                       .then_inc(sg["m_masked"], 1)
                    dve.wait_ge(sg["m_masked"], h + 1)
                    dve.reduce_max(m_mx[:, 0:1], m_s[:, 0:P], AX_X)
                    dve.reduce_max(m_mx[:, 1:2], m_s[:, P:3 * P], AX_X).then_inc(sg["m_max"], 1)
                    dve.wait_ge(sg["m_max"], h + 1)
                    dve.tensor_scalar(m_mx[:, 2:4], m_mx[:, 0:2], -SCALE, None, ALU.mult).then_inc(sg["m_bias"], 1)
                    dve.wait_ge(sg["m_exp"], h + 1)
                    dve.reciprocal(m_mx[:, 6:8], m_mx[:, 4:6]).then_inc(sg["m_rinv"], 1)
                    dve.wait_ge(sg["m_rinv"], h + 1)
                    dve.tensor_scalar(m_s[:, 0:P], m_s[:, 0:P], m_mx[:, 6:7], None, ALU.mult)
                    dve.tensor_scalar(m_s[:, P:3 * P], m_s[:, P:3 * P], m_mx[:, 7:8], None, ALU.mult)\
                       .then_inc(sg["m_prob"], 1)
                if j == 3:
                    dve.wait_ge(sg["m_hi"], h + 1)
                    dve.tensor_tensor(ya[:, bass.ds(h, 1), 1, :].rearrange("p o t -> p (o t)"), ps[:, 6, SEQ:2 * SEQ],
                                      ya[:, bass.ds(h, 1), 0, :].rearrange("p o t -> p (o t)").bitcast(F32),
                                      ALU.subtract).then_inc(sg["m_free"], 1)

            def conv(dve, it, g, p, use):
                add_halves(dve, p, use, cin[:, :, TAPS - 1:TAPS - 1 + SEQ])
                w = S_CONV + g * HEADS * TAPS
                for tap in range(1, TAPS):
                    for c in range(2):
                        if tap == 1:
                            read_out(dve, p, use)
                            dve.wait_ge(sg["c_tap"], (it * 3 + g) * 2 + c + 1)
                        else:
                            dve.wait_ge(sg["c_acc"], (it * 3 + g) * 4 + tap * 2 + c - 3)
                        last = tap == TAPS - 1
                        dest = dn[:, bass.ds(it * 2 + c, 1), g, :].rearrange("p o t -> p (o t)") if last \
                            else cacc[:, c, :]
                        ins = dve.scalar_tensor_tensor(out=dest, in0=cin[:, c, tap:tap + SEQ],
                                                       scalar=par[:, bass.ds(w + (it * 2 + c) * TAPS + tap, 1)],
                                                       in1=cacc[:, c, :], op0=ALU.mult, op1=ALU.add)
                        if not last:
                            ins.then_inc(sg["c_acc"], 1)
                ins.then_inc(sg["c_sum"], 1)

            read_out(dve, 1, U_IN2 - 1)
            dve.wait_ge(sg["c_zero"], 1)
            with dve.Fori(0, 4) as it:
                for m in range(12):
                    split(dve, T_IN2 + it * 3 + m // 4, m % 4)
                    for j in range(8):
                        if MOBA_AT[j] // 4 == m:
                            moba_reply(dve, j % 4, it * 2 + j // 4)
                    if m in (4, 8):
                        conv(dve, it, m // 4 - 1, m // 4 - 1, it + U_IN2)
                conv(dve, it, 2, 2, it)

            def head_norm(dve, h):
                dve.wait_ge(sg["d_rstd"], h + 1)
                dve.scalar_tensor_tensor(out=d_qn[:, :], in0=dn[:, bass.ds(h, 1), 0, :].rearrange("p o t -> p (o t)"),
                                         scalar=SCALE, in1=d_sq[:, 0, :], op0=ALU.mult, op1=ALU.mult)
                dve.tensor_tensor(d_kn[:, :], dn[:, bass.ds(h, 1), 1, :].rearrange("p o t -> p (o t)"), d_sq[:, 1, :],
                                  ALU.mult).then_inc(sg["d_norm"], 1)

            head_norm(dve, 0)
            with dve.Fori(0, HEADS) as h:
                def step(m):
                    split(dve, T_IN3 + h * 2 + m // 4, m % 4)

                dve.wait_ge(sg["d_rows"], h + 1)
                dve.wait_ge(sg["d_norm"], h + 1)
                dve.wait_ge(sg["d_free"], h + 1)
                dve.tensor_tensor(d_kb[:, :], d_kn[:, :], ps[:, 5, SEQ:2 * SEQ], ALU.mult).then_inc(sg["d_kb_ready"], 1)
                for t in range(TOK):
                    ins = dve.tensor_scalar(d_e[:, t, :], ps[:, 5, t * P:(t + 1) * P], gcol[:, t, 2, bass.ds(h, 1)], 0.0,
                                            ALU.subtract, ALU.min)
                ins.then_inc(sg["d_arg"], 1)
                step(0)
                step(1)
                dve.wait_ge(sg["d_prod"], h + 1)
                dve.wait_ge(sg["d_exp"], h + 1)
                dve.tensor_tensor(d_vn[:, :, :], ps[:, 7, 0:SEQ].rearrange("p (t d) -> p t d", t=TOK), d_e[:, :, :],
                                  ALU.mult).then_inc(sg["d_amat"], 1)
                dve.wait_ge(sg["d_amat"], h + 1)
                dve.tensor_tensor(d_lv[:, 0], d_vn[:, :, :], per_tile(con[:, C_LEVEL:C_LEVEL + P]), ALU.mult)\
                   .then_inc(sg["d_lv0_ready"], 1)
                dve.wait_ge(sg["d_incl"], h + 1)
                dve.tensor_tensor(d_at[:, :, :], ps[:, 7, SEQ:2 * SEQ].rearrange("p (t d) -> p t d", t=TOK),
                                  d_p[:, :, :], ALU.mult).then_inc(sg["d_attn"], 1)
                dve.wait_ge(sg["d_lv0_ready"], h + 1)
                dve.tensor_tensor(d_tu[:, 1], per_tile(ident), d_lv[:, 0], ALU.subtract).then_inc(sg["d_u_level"], 1)
                dve.wait_ge(sg["d_l0"], h + 1)
                dve.tensor_tensor(d_tu[:, 0], per_tile(ident), ps[:, 4, 0:SEQ].rearrange("p (t d) -> p t d", t=TOK),
                                  ALU.subtract).then_inc(sg["d_t_ready"], 1)
                for j in range(1, LEVELS):
                    if j < LEVELS - 1:
                        dve.wait_ge(sg["d_tp_done"], h * (LEVELS - 2) + j)
                        dve.tensor_tensor(d_tu[:, 0], d_tu[:, 0], ps[:, 5, 0:SEQ].rearrange("p (t d) -> p t d", t=TOK),
                                          ALU.subtract).then_inc(sg["d_t_ready"], 1)
                    dve.wait_ge(sg["d_pu_done"], h * (LEVELS - 1) + j)
                    dve.tensor_tensor(d_tu[:, 1], d_tu[:, 1], ps[:, 7, SEQ:2 * SEQ].rearrange("p (t d) -> p t d", t=TOK),
                                      ALU.subtract).then_inc(sg["d_u_level"], 1)
                    if j in (1, 2, 4, 5):
                        step({1: 2, 2: 3, 4: 4, 5: 5}[j])
                dve.wait_ge(sg["d_kbg_ready"], (h + 1) * TOK)
                for t in range(TOK):
                    ins = dve.tensor_scalar(d_kd[:, t, :], ps[:, 6, t * P:(t + 1) * P], gcol[:, t, 4, bass.ds(h, 1)],
                                            None, ALU.mult)
                ins.then_inc(sg["d_kd_ready"], 1)
                add_halves(dve, 0, U_IN3 + h, gates[:, bass.ds(h * 4, 2), :])
                step(6)
                dve.wait_ge(sg["d_u_ready"], h + 1)
                dve.wait_ge(sg["d_levels"], (h + 1) * (LEVELS - 1))
                for c in range(NCH):
                    t, o = c // 2, (c % 2) * CHUNK
                    if c == 0:
                        dve.tensor_copy(d_vn[o:o + CHUNK, t, :], d_uw[o:o + CHUNK, 0, t, :]).then_inc(sg["d_vn_ready"], 1)
                    else:
                        dve.wait_ge(sg["d_ws"], h * (NCH - 1) + c)
                        dve.tensor_tensor(d_vn[o:o + CHUNK, t, :], d_uw[o:o + CHUNK, 0, t, :], ps[o:o + CHUNK, 4, 0:P],
                                          ALU.subtract).then_inc(sg["d_vn_ready"], 1)
                    dve.wait_ge(sg["d_okv"], h * NCH + c + 1)
                    if c == 0:
                        dve.tensor_copy(d_state[:, :], ps[:, 5, 0:P]).then_inc(sg["d_state_ready"], 1)
                    elif c < NCH - 1:
                        dve.scalar_tensor_tensor(out=d_state[:, :], in0=d_state[:, :],
                                                 scalar=glast[:, c, bass.ds(h, 1)], in1=ps[:, 5, 0:P], op0=ALU.mult,
                                                 op1=ALU.add).then_inc(sg["d_state_ready"], 1)
                step(7)
                head_norm(dve, h + 1)
                dve.wait_ge(sg["d_orstd"], h + 1)
                dve.scalar_tensor_tensor(out=d_kb[:, :], in0=ps[:, 6, 0:SEQ], scalar=par[:, S_OG:S_OG + 1],
                                         in1=d_on[:, 1, :], op0=ALU.mult, op1=ALU.mult).then_inc(sg["d_on"], 1)
                dve.wait_ge(sg["d_on"], h + 2)
                dve.tensor_tensor(d_kb[:, :], d_kb[:, :], z[:, bass.ds(h, 1), :].rearrange("p o t -> p (o t)"), ALU.mult)\
                   .then_inc(sg["d_y"], 1)
                dve.wait_ge(sg["d_y"], h + 1)
                dve.tensor_scalar(yb[:, bass.ds(h, 1), 0, :].rearrange("p o t -> p (o t)"), d_kb[:, :], 1.0, None, ALU.mult)\
                   .then_inc(sg["d_yhi"], 1)
                dve.wait_ge(sg["d_yhi"], h + 1)
                dve.tensor_tensor(yb[:, bass.ds(h, 1), 1, :].rearrange("p o t -> p (o t)"), d_kb[:, :],
                                  yb[:, bass.ds(h, 1), 0, :].rearrange("p o t -> p (o t)").bitcast(F32), ALU.subtract)\
                   .then_inc(sg["d_free"], 1)
                add_halves(dve, 1, U_IN3 + h, gates[:, bass.ds(h * 4 + 2, 2), :])

            sig = mg[:, 0:2, :].rearrange("p a (b t) -> p a b t", t=SEQ)
            prod = mg[:, 2:4, :].rearrange("p a (b t) -> p a b t", t=SEQ)

            def merged_lo(dve, g):
                dve.wait_ge(sg["g_hi"], g + 1)
                dve.tensor_tensor(hs[:, bass.ds(g * 2, 2), 1, :], prod[:, 0], hs[:, bass.ds(g * 2, 2), 0, :].bitcast(F32),
                                  ALU.subtract).then_inc(sg["g_merged"], 1)

            def merge_group(dve, g, follows):
                for s in range(SLOTS):
                    split(dve, T_MRG + g, s)
                    if s == 0 and follows:
                        merged_lo(dve, g - 1)
                    if s == 2:
                        dve.wait_ge(sg["g_merged"], g + 1)
                        branch(dve, g, 0)
                branch(dve, g, 1)
                dve.wait_ge(sg["g_mul"], g * 2 + 2)
                dve.tensor_tensor(prod[:, 0], prod[:, 0], prod[:, 1], ALU.add).then_inc(sg["merged"], 1)

            def branch(dve, g, j):
                add_halves(dve, j, U_MRG + g, prod[:, j])
                read_out(dve, j, U_MRG + g)
                dve.wait_ge(sg["g_sig"], g * 2 + j + 1)
                dve.tensor_tensor(prod[:, j], prod[:, j], sig[:, j], ALU.mult).then_inc(sg["g_mul"], 1)

            merge_group(dve, 0, False)
            with dve.Fori(1, 8) as g:
                merge_group(dve, g, True)
            merged_lo(dve, 7)

            def residual(p, turn, s, col, done):
                multiplied(dve, turn, s)
                for t, signal in enumerate((done, pair_free[p])):
                    part = x1[:, t, bass.ds(col, 512)]
                    dve.tensor_tensor(part, part, ps[:, 2 * p + t, :], ALU.add).then_inc(signal, 1)
            with dve.Fori(0, 2) as it:
                for p in range(2):
                    for s in range(8):
                        split(dve, T_OUT + it * 4 + p * 2 + s // 4, s % 4)
                        if p == 1 and s == 2:
                            dve.wait_ge(x1_loaded, 16)
                            residual(0, T_OUT + it * 4 + 1, 3, it * 1024, sg["x1_added"])
                residual(1, T_OUT + it * 4 + 3, 3, it * 1024 + 512, sg["x1_added"])
            dve.wait_ge(sg["x1_sq"], 9)
            dve.reduce_sum(rstat[:, 4, :], rstat[:, 0:4, :].rearrange("p a t -> p t a"), AX_X)\
               .then_inc(sg["stat_sum"], 1)
            norm_dve(dve, 1, S_FFN, x1, scaled, T_FFN, {5: 2, 10: 3})

            dve.memset(fin[:, :, 0:FTAPS - 1], 0.0).then_inc(sg["f_zero"], 1)
            def ffn_group(dve, g, made=0):
                for m in range(8):
                    if m >= made:
                        split(dve, T_FFN + g * 2 + m // 4, m % 4)
                    if m == 4:
                        add_halves(dve, 0, U_FFN + g, fin[:, :, FTAPS - 1:FTAPS - 1 + SEQ], U_FFN - U_OUT)
                        for tap in range(1, FTAPS):
                            for c in range(2):
                                if tap == 1:
                                    read_out(dve, 0, U_FFN + g)
                                    dve.wait_ge(sg["f_tap"], g * 2 + c + 1)
                                else:
                                    dve.wait_ge(sg["f_acc"], g * 4 + c + 1)
                                dve.scalar_tensor_tensor(
                                    out=facc[:, c, :], in0=fin[:, c, tap:tap + SEQ],
                                    scalar=par[:, bass.ds(S_FCONV + (g * 2 + c) * FTAPS + tap, 1)],
                                    in1=facc[:, c, :], op0=ALU.mult, op1=ALU.add).then_inc(sg["f_acc"], 1)
                fup = fin[:, :, FTAPS - 1:FTAPS - 1 + SEQ]
                add_halves(dve, 1, U_FFN + g, fup, U_FFN - U_OUT)
                read_out(dve, 1, U_FFN + g)
                dve.wait_ge(sg["f_silu"], g + 1)
                dve.tensor_tensor(facc[:, :, :], facc[:, :, :], fup, ALU.mult).then_inc(sg["f_prod"], 1)
                dve.wait_ge(sg["f_hi"], g + 1)
                dve.tensor_tensor(act_s[:, bass.ds(g * 2, 2), 1, :], facc[:, :, :],
                                  act_s[:, bass.ds(g * 2, 2), 0, :].bitcast(F32), ALU.subtract)\
                   .then_inc(sg["hidden_ready"], 1)

            ffn_group(dve, 0, SLOTS - AHEAD_LO)
            with dve.Fori(1, 22) as g:
                ffn_group(dve, g)

            for cb in range(4):
                for j in range(22):
                    n = cb * 22 + j
                    if n < 88 - AHEAD_LO:
                        split(dve, T_DWN + n // 4, n % 4)
                    if j == 4 and cb > 0:
                        last = cb * 22 - 1
                        residual((cb - 1) % 2, T_DWN + last // 4, last % 4, (cb - 1) * 512, sg["y_added"])
            residual(1, TURNS - 1, 3, 3 * 512, sg["y_added"])

        @block.tensor
        def _(pe):
            pe.wait_ge(first_loaded, 32)
            norm_pe(pe, 0, xt, T_IN1, U_IN1)

            def in1_group(pe, it, p):
                channel_group(pe, T_IN1 + it * 2 + p, p, U_IN1 + it, hs)
            in1_group(pe, 0, 1)
            with pe.Fori(1, 6) as it:
                for p in range(2):
                    in1_group(pe, it, p)
            pe.wait_ge(ba_lo, 1)
            bank = ps[0:2 * HEADS, 6, :]
            for k in range(KD):
                last = k == KD - 1
                for lo in ((False, True), (True, False))[last]:
                    if lo:
                        pe.matmul(bank[:, 0:SEQ], wbal[:, k, :], hs[:, k, 0, :], start=False, stop=False,
                                  skip_group_check=True)
                    else:
                        mm = pe.matmul(bank, wbah[:, k, :], hs[:, k, :, :].rearrange("p a t -> p (a t)"), start=k == 0,
                                       stop=last)
            mm.then_inc(ba_done, 1)
            in1_group(pe, 6, 0)
            pe.wait_ge(ba_added, 1)
            for t in range(TOK):
                mm = pe.transpose(ps[:, 6, t * 2 * HEADS:(t + 1) * 2 * HEADS], ba[0:2 * HEADS, 0, t * P:(t + 1) * P],
                                  ident[0:2 * HEADS, 0:2 * HEADS])
            mm.then_inc(ba_turned, 1)
            in1_group(pe, 6, 1)
            in1_group(pe, 7, 0)
            pe.wait_ge(gate_v, 4)
            pe.wait_ge(ones_set, 1)
            pe.wait_ge(tables_loaded, 32)
            same, up = con[:, C_SAME:C_SAME + P], con[:, C_UP:C_UP + P]
            for t in range(TOK):
                g_t = gcol[:, t, 0, :]
                pe.matmul(ps[:, 7, t * HEADS:(t + 1) * HEADS], up, g_t, start=True, stop=True)
                pe.matmul(ps[:, 7, 32 + t * HEADS:32 + (t + 1) * HEADS], same, g_t, start=True, stop=True)
                for o in range(2):
                    c = 2 * t + o
                    mm = pe.matmul(ps[:, 7, 64 + c * HEADS:64 + (c + 1) * HEADS],
                                   con[:, C_HALF + o * P:C_HALF + (o + 1) * P], g_t, start=True, stop=True)
            mm.then_inc(gate_sums, 1)
            in1_group(pe, 7, 1)

            def moba_step(pe, j, h):
                if j == 0:
                    pe.wait_ge(sg["m_squares"], h + 1)
                    pe.wait_ge(sg["m_free"], h + 1)
                    pe.matmul(ps[:, 6, :], ones[:, :], m_sq[:, :, :].rearrange("p a t -> p (a t)"), start=True,
                              stop=True).then_inc(sg["m_ssq"], 1)
                if j == 1:
                    pe.wait_ge(sg["m_qn_ready"], h + 1)
                    pe.matmul(ps[:, 7, 0:P], m_qn[:, 0:P], m_kn[:, 0:P], start=True, stop=True)
                    pe.matmul(ps[:, 7, P:3 * P], m_qn[:, P:2 * P], m_kn[:, :], start=True, stop=True)\
                      .then_inc(sg["m_scores"], 1)
                    pe.wait_ge(sg["m_v_ready"], h + 1)
                    for t in range(TOK):
                        mm = pe.transpose(ps[:, 6, t * P:(t + 1) * P], m_v[:, t * P:(t + 1) * P], ident)
                    mm.then_inc(sg["m_vturned"], 1)
                if j == 2:
                    pe.wait_ge(sg["m_prob"], h + 1)
                    for i in range(3):
                        mm = pe.transpose(ps[:, 7, i * P:(i + 1) * P], m_s[:, i * P:(i + 1) * P], ident)
                    mm.then_inc(sg["m_pturned"], 1)
                if j == 3:
                    pe.wait_ge(sg["m_pt_ready"], h + 1)
                    pe.wait_ge(sg["m_vt_ready"], h + 1)
                    pe.matmul(ps[:, 6, SEQ:SEQ + P], m_vt[:, 0, :], m_pt[:, 0:P], start=True, stop=True)
                    pe.matmul(ps[:, 6, SEQ + P:2 * SEQ], m_vt[:, 0, :], m_pt[:, P:2 * P], start=True, stop=False)
                    pe.matmul(ps[:, 6, SEQ + P:2 * SEQ], m_vt[:, 1, :], m_pt[:, 2 * P:3 * P], start=False,
                              stop=True).then_inc(sg["m_out"], 1)

            pe.wait_ge(gates_ready, 2)
            with pe.Fori(0, 4) as it:
                for i in range(48):
                    if i in MOBA_AT:
                        j = MOBA_AT.index(i)
                        moba_step(pe, j % 4, it * 2 + j // 4)
                    g = i // 16
                    channel_unit(pe, T_IN2 + it * 3 + g, i // 4 % 4, i % 4, g, it + (U_IN2 if g < 2 else 0), hs, i % 16,
                                 i % 16 == 0, i % 16 == 15)

            pe.wait_ge(pair_free[2], 5)
            pe.wait_ge(sg["m_free"], HEADS + 1)
            def head_ssq(h):
                pe.wait_ge(sg["d_squares"], h + 1)
                pe.matmul(ps[:, 7, :], ones[:, :], d_sq[:, :, :].rearrange("p a t -> p (a t)"), start=True, stop=True)\
                  .then_inc(sg["d_ssq"], 1)

            head_ssq(0)
            with pe.Fori(0, HEADS) as h:
                def fill(step):
                    for i in range(sum(FILL[:step]), sum(FILL[:step + 1])):
                        g = i // 16
                        channel_unit(pe, T_IN3 + h * 2 + g, i // 4 % 4, i % 4, g, U_IN3 + h, hs, i % 16, i % 16 == 0,
                                     i % 16 == 15)

                def both(out, lhs, rhs, col=0):
                    for t in range(TOK):
                        mm = pe.matmul(ps[:, out, col + t * P:col + (t + 1) * P], lhs(t), rhs(t), start=True, stop=True)
                    return mm

                pe.wait_ge(sg["d_cast_ready"], h + 1)
                both(5, lambda t: d_cast[:, 0, t, :], lambda t: up)
                both(5, lambda t: d_cast[:, 1, t, :], lambda t: ident, SEQ).then_inc(sg["d_rows"], 1)
                fill(1)
                pe.wait_ge(sg["d_on"], h + 1)
                pe.wait_ge(sg["d_norm"], h + 1)
                pe.wait_ge(sg["d_v_ready"], h + 1)
                for t in range(TOK):
                    pe.transpose(ps[:, 6, t * P:(t + 1) * P], d_kn[:, t * P:(t + 1) * P], ident)
                    mm = pe.transpose(ps[:, 6, SEQ + t * P:SEQ + (t + 1) * P], d_v[:, t * P:(t + 1) * P], ident)
                mm.then_inc(sg["d_tok"], 1)
                fill(2)
                pe.wait_ge(sg["d_kb_ready"], h + 1)
                both(7, lambda t: d_kn[:, t * P:(t + 1) * P], lambda t: d_kb[:, t * P:(t + 1) * P])
                both(7, lambda t: d_kn[:, t * P:(t + 1) * P], lambda t: d_qn[:, t * P:(t + 1) * P], SEQ)\
                    .then_inc(sg["d_prod"], 1)
                fill(3)
                pe.wait_ge(sg["d_lv0_ready"], h + 1)
                both(4, lambda t: d_lv[:, 0, t, :], lambda t: ident).then_inc(sg["d_l0"], 1)
                fill(4)
                for j in range(1, LEVELS):
                    pe.wait_ge(sg["d_levels"], h * (LEVELS - 1) + j)
                    pe.wait_ge(sg["d_t_ready"], h * (LEVELS - 1) + j)
                    if j == 1:
                        pe.wait_ge(sg["d_attn"], h + 1)
                    both(4, lambda t: d_lv[:, j, t, :], lambda t: d_tu[:, 0, t, :]).then_inc(sg["d_p_done"], 1)
                    fill(3 + 2 * j)
                    pe.wait_ge(sg["d_p_ready"], h * (LEVELS - 1) + j)
                    if j == 1:
                        pe.wait_ge(sg["d_egrow"], h + 1)
                    pe.wait_ge(sg["d_u_level"], h * LEVELS + j)
                    if j < LEVELS - 1:
                        both(5, lambda t: d_tu[:, 1, t, :], lambda t: d_p[:, t, :]).then_inc(sg["d_tp_done"], 1)
                    both(7, lambda t: d_p[:, t, :], lambda t: d_tu[:, 1, t, :], SEQ).then_inc(sg["d_pu_done"], 1)
                    fill(4 + 2 * j)
                pe.wait_ge(sg["d_u_level"], (h + 1) * LEVELS)
                pe.wait_ge(sg["d_vb_ready"], (h + 1) * TOK)
                pe.wait_ge(sg["d_kbg_ready"], (h + 1) * TOK)
                both(7, lambda t: d_tu[:, 1, t, :], lambda t: d_vb[:, t, :])
                both(7, lambda t: d_kbg[:, t, :], lambda t: d_tu[:, 1, t, :], SEQ).then_inc(sg["d_uw"], 1)
                fill(15)
                pe.wait_ge(sg["d_u_ready"], h + 1)
                pe.wait_ge(sg["d_qg_ready"], h + 1)
                pe.wait_ge(sg["d_kd_ready"], h + 1)
                for c in range(NCH):
                    t, o = c // 2, (c % 2) * CHUNK
                    if c > 0:
                        pe.wait_ge(sg["d_state_ready"], h * (NCH - 1) + c)
                        pe.matmul(ps[o:o + CHUNK, 4, 0:P], d_uw[:, 1, t, o:o + CHUNK], d_state[:, :], start=True,
                                  stop=True).then_inc(sg["d_ws"], 1)
                        fill(15 + 2 * c)
                    pe.wait_ge(sg["d_vn_ready"], h * NCH + c + 1)
                    dst = ps[:, 6, c * CHUNK:(c + 1) * CHUNK]
                    if c > 0:
                        pe.matmul(dst, d_state[:, :], d_qg[:, c * CHUNK:(c + 1) * CHUNK], start=True, stop=False)
                    mm = pe.matmul(dst, d_vn[o:o + CHUNK, t, :], d_at[o:o + CHUNK, t, o:o + CHUNK], start=c == 0,
                                   stop=True)
                    if c < NCH - 1:
                        mm = pe.matmul(ps[:, 5, 0:P], d_kd[o:o + CHUNK, t, :], d_vn[o:o + CHUNK, t, :], start=True,
                                       stop=True)
                    mm.then_inc(sg["d_okv"], 1)
                    if c == 1:
                        head_ssq(h + 1)
                    fill(16 + 2 * c)
                pe.wait_ge(sg["d_osq"], h + 1)
                pe.matmul(ps[:, 7, 0:SEQ], ones[:, :], d_on[:, 0, :], start=True, stop=True).then_inc(sg["d_ossq"], 1)
                fill(23)

            pe.wait_ge(sg["m_free"], HEADS + 1)
            with pe.Fori(0, 8) as g:
                channel_group(pe, T_MRG + g, 0, U_MRG + g, ya, (0, 1))
                pe.wait_ge(sg["d_free"], HEADS + 1)
                channel_group(pe, T_MRG + g, 1, U_MRG + g, yb, (2, 3))

            pe.wait_ge(sg["g_merged"], 8)
            with pe.Fori(0, 2) as it:
                for p in range(2):
                    for s in range(8):
                        if p == 0 and s == 7:
                            pe.wait_ge(sg["g_merged"], 9)
                        token_slab(pe, T_OUT + it * 4 + p * 2 + s // 4, s % 4, p, U_OUT + it, hs, 2 * s, s == 0, s == 7)

            norm_pe(pe, 1, scaled, T_FFN, U_FFN)
            channel_group(pe, T_FFN + 1, 1, U_FFN, hs)
            with pe.Fori(1, 22) as g:
                channel_group(pe, T_FFN + g * 2, 0, U_FFN + g, hs)
                channel_group(pe, T_FFN + g * 2 + 1, 1, U_FFN + g, hs)

            pe.wait_ge(sg["hidden_ready"], 21)
            with pe.Fori(0, 2) as it:
                for n in range(44):
                    j = n % 22
                    if n == 21:
                        pe.wait_ge(sg["hidden_ready"], 22)
                    token_slab(pe, T_DWN + it * 11 + n // 4, n % 4, n // 22, U_DWN + it, act_s, 2 * j, j == 0, j == 21)


def _slabs(w, rows, cols):
    k, n = w.shape
    v = w.reshape(k // (P * rows), rows, P, n // cols, cols)
    return v.transpose(3, 0, 2, 1, 4).reshape(n // cols, k // (P * rows), P, rows * cols)


def _constants(np):
    c = np.zeros((P, C_ALL), np.float32)
    i, j = np.arange(P)[:, None], np.arange(P)[None, :]
    chunk = i // CHUNK == j // CHUNK
    c[:, C_ID:C_ID + P] = i == j
    c[:, C_UP:C_UP + P] = chunk & (i <= j)
    c[:, C_SAME:C_SAME + P] = chunk
    for o in range(2):
        c[:, C_HALF + o * P:C_HALF + (o + 1) * P] = i // CHUNK == o
    for n in range(LEVELS):
        b = 1 << n
        c[:, C_LEVEL + n * P:C_LEVEL + (n + 1) * P] = (i // (2 * b) == j // (2 * b)) & (i % (2 * b) < b) & (j % (2 * b) >= b)
    causal = np.where(j <= i, 0.0, -1e30)
    c[:, C_CAUSAL:C_CAUSAL + P] = causal
    c[:, C_CAUSAL + 2 * P:C_CAUSAL + 3 * P] = causal
    return c


def kernel(**inputs):
    import numpy as np
    import concourse.bacc as bacc
    from concourse.bass_utils import run_bass_kernel_spmd

    a = {k: np.asarray(v) for k, v in inputs.items()}
    w_in, w_ffn = a["w_in"][0], a["w_ffn_in"][0]
    heads = HEADS * HD
    z0, b0, g0 = 6 * heads, 7 * heads, 7 * heads + 2 * HEADS
    flat = (-1, P, SLAB)

    def columns(v, n):
        return np.moveaxis(v.reshape(-1, n, P), 2, 0).transpose(0, 2, 1)

    in_slabs = [_slabs(w_in[:, c:c + n], 4, 256) for c, n in
                ((0, 3 * heads), (z0, heads), (3 * heads, 3 * heads), (g0, 2 * D))]
    dn = in_slabs[2].reshape(3, 4, 4, P, SLAB).transpose(1, 0, 2, 3, 4)
    branch = np.stack([_slabs(a["w_branch_a"][0], 4, 256), _slabs(a["w_branch_b"][0], 4, 256)], axis=1)
    gate, up = _slabs(w_ffn[:, :FF], 4, 256), _slabs(w_ffn[:, FF:], 4, 256)
    stream = np.concatenate([in_slabs[0].reshape(flat), in_slabs[1].reshape(flat), dn.reshape(flat),
                             in_slabs[3].reshape(flat), branch.reshape(flat),
                             _slabs(a["w_out"][0], 2, 512).reshape(flat),
                             np.stack([gate, up], axis=1).reshape(flat),
                             _slabs(a["w_ffn_down"][0], 2, 512).reshape(flat)])
    small = np.concatenate([
        a["attn_norm"][0].reshape(KD, P).T, a["ffn_norm"][0].reshape(KD, P).T,
        a["moba_q_norm"].reshape(P, 1), a["moba_k_norm"].reshape(P, 1), a["dn_out_norm"].reshape(P, 1),
        np.repeat(a["dn_a_log"].reshape(1, HEADS), P, axis=0), np.repeat(a["dn_dt_bias"].reshape(1, HEADS), P, axis=0),
        columns(a["dn_conv"][0], 3 * HEADS).reshape(P, -1), columns(a["ffn_conv"][0], KF).reshape(P, -1),
        a["ffn_conv_bias"][0].reshape(KF, P).T], axis=1)
    arrays = {
        "x": np.ascontiguousarray(a["x"][0]),
        "stream": np.ascontiguousarray(stream),
        "w_ba": np.ascontiguousarray(w_in[:, b0:g0].reshape(KD, P, 2 * HEADS).transpose(1, 0, 2)),
        "consts": _constants(np),
        "small": np.ascontiguousarray(small),
    }
    nc = bacc.Bacc("TRN2", target_bir_lowering=False, num_devices=1)
    args = [nc.dram_tensor(f"in_{n}", v.shape, F32, kind="ExternalInput").ap() for n, v in arrays.items()]
    out = nc.dram_tensor("out", (SEQ, D), F32, kind="ExternalOutput").ap()
    layer(nc, *args, out)
    r = run_bass_kernel_spmd(nc, [{f"in_{n}": v for n, v in arrays.items()}], core_ids=[0])
    return r.results[0]["out"].reshape(1, SEQ, D)
```
